# Optimizing a Trainium2 kernel written in Bass

```python
import jax, jax.numpy as jnp
from jax import lax
import numpy as np
import math

D_MODEL = 1024
BATCH = 1
SEQ = 256
DEPTH = 1

FOURIER_GROUPS = 4
FOURIER_GROUP_DIM = 128
D_FOURIER = FOURIER_GROUPS * FOURIER_GROUP_DIM
D_CONV = D_MODEL
CONV_WIDTH = 3
N_BRANCHES = 2
D_IN_PROJ = D_FOURIER + 3 * D_CONV + N_BRANCHES * D_MODEL
N_EXPERTS = 16
EC_CAPACITY = 2
D_EXPERT = 2048
N_MOD = 6
RMS_EPS = 1e-6


def rms_norm(x, g):
    xf = x.astype(jnp.float32)
    y = xf * lax.rsqrt(jnp.mean(xf * xf, axis=-1, keepdims=True) + RMS_EPS)
    return (y * g.astype(jnp.float32)).astype(x.dtype)

def modulate(h, shift, scale):
    return h * (1 + scale[:, None, :]) + shift[:, None, :]

def fourier_mix(u):
    b, s, _ = u.shape
    ug = u.reshape(b, s, FOURIER_GROUPS, FOURIER_GROUP_DIM).astype(jnp.float32)
    f = jnp.fft.fftn(ug, axes=(1, 3), norm="ortho")
    return jnp.real(f).reshape(b, s, D_FOURIER).astype(u.dtype)

def centred_conv3(u, w):
    s = u.shape[1]
    up = jnp.pad(u, ((0, 0), (1, 1), (0, 0)))
    return up[:, 0:s] * w[0] + up[:, 1:s + 1] * w[1] + up[:, 2:s + 2] * w[2]

def expert_choice_moe(h, w_router, b_router, w_gate_e, w_up_e, w_down_e):
    b, s, d = h.shape
    cap = EC_CAPACITY * s // N_EXPERTS
    logits = jnp.einsum('bsd,de->bse', h, w_router).astype(jnp.float32) + b_router.astype(jnp.float32)
    probs = jax.nn.softmax(logits, axis=-1)
    vals, idx = lax.top_k(jnp.swapaxes(probs, 1, 2), cap)
    xe = jax.vmap(lambda hb, ib: hb[ib])(h, idx)
    a = jnp.einsum('becd,edf->becf', xe, w_gate_e)
    u = jnp.einsum('becd,edf->becf', xe, w_up_e)
    y = jnp.einsum('becf,efd->becd', jax.nn.silu(a) * u, w_down_e)
    y = y * vals[..., None].astype(y.dtype)
    return jax.vmap(lambda yb, ib: jnp.zeros((s, d), yb.dtype).at[ib.reshape(-1)].add(yb.reshape(-1, d)))(y, idx)

def first_inputs(seed: int = 0) -> dict:
    key = jax.random.key(seed)
    ks = jax.random.split(key, 20)
    f32 = jnp.float32
    nrm = lambda k, shape, scale: (jax.random.normal(k, shape, f32) * scale).astype(f32)
    D = D_MODEL
    return {
        "x": nrm(ks[0], (BATCH, SEQ, D), 1.0),
        "c": nrm(ks[1], (BATCH, D), 1.0),
        "w_ada": nrm(ks[2], (DEPTH, D, N_MOD * D), 0.5 * D ** -0.5),
        "b_ada": nrm(ks[3], (DEPTH, N_MOD * D), 0.02),
        "g_norm_mix": 1.0 + nrm(ks[4], (DEPTH, D), 0.02),
        "w_in": nrm(ks[5], (DEPTH, D, D_IN_PROJ), D ** -0.5),
        "b_gate": nrm(ks[6], (DEPTH, N_BRANCHES * D), 0.02),
        "w_fourier": nrm(ks[7], (DEPTH, D_FOURIER, D), D_FOURIER ** -0.5),
        "w_conv": nrm(ks[8], (DEPTH, CONV_WIDTH, D_CONV), CONV_WIDTH ** -0.5),
        "w_conv_out": nrm(ks[9], (DEPTH, D_CONV, D), D_CONV ** -0.5),
        "w_o": nrm(ks[10], (DEPTH, D, D), D ** -0.5),
        "g_norm_moe": 1.0 + nrm(ks[11], (DEPTH, D), 0.02),
        "w_router": nrm(ks[12], (DEPTH, D, N_EXPERTS), D ** -0.5),
        "b_router": nrm(ks[13], (DEPTH, N_EXPERTS), 0.01),
        "w_gate_e": nrm(ks[14], (DEPTH, N_EXPERTS, D, D_EXPERT), D ** -0.5),
        "w_up_e": nrm(ks[15], (DEPTH, N_EXPERTS, D, D_EXPERT), D ** -0.5),
        "w_down_e": nrm(ks[16], (DEPTH, N_EXPERTS, D_EXPERT, D), D_EXPERT ** -0.5),
        "g_final": 1.0 + nrm(ks[17], (D,), 0.02),
    }

def first_block(x, c, w_ada, b_ada, g_norm_mix, w_in, b_gate, w_fourier, w_conv, w_conv_out, w_o,
              g_norm_moe, w_router, b_router, w_gate_e, w_up_e, w_down_e, g_final):
    D = D_MODEL
    c_act = jax.nn.silu(c)
    for l in range(DEPTH):
        mod = jnp.einsum('bd,dm->bm', c_act, w_ada[l]) + b_ada[l]
        shift_m, scale_m, gate_m, shift_f, scale_f, gate_f = jnp.split(mod, N_MOD, axis=-1)

        h = modulate(rms_norm(x, g_norm_mix[l]), shift_m, scale_m)
        p = jnp.einsum('bsd,dk->bsk', h, w_in[l])
        o1 = D_FOURIER
        o2 = o1 + D_CONV
        o3 = o2 + D_CONV
        o4 = o3 + D_CONV
        u_f = p[..., :o1]
        v, b_g, c_g = p[..., o1:o2], p[..., o2:o3], p[..., o3:o4]
        g_logits = p[..., o4:] + b_gate[l]
        gate_a = jax.nn.sigmoid(g_logits[..., :D])
        gate_b = jax.nn.sigmoid(g_logits[..., D:])
        y_a = jnp.einsum('bsk,kd->bsd', fourier_mix(u_f), w_fourier[l])
        y_b = jnp.einsum('bsk,kd->bsd', b_g * centred_conv3(c_g * v, w_conv[l]), w_conv_out[l])
        z = gate_a * y_a + gate_b * y_b
        mix_out = jnp.einsum('bsd,de->bse', z, w_o[l])
        x = x + gate_m[:, None, :] * mix_out

        h2 = modulate(rms_norm(x, g_norm_moe[l]), shift_f, scale_f)
        moe_out = expert_choice_moe(h2, w_router[l], b_router[l], w_gate_e[l], w_up_e[l], w_down_e[l])
        x = x + gate_f[:, None, :] * moe_out
    return rms_norm(x, g_final)


PLE_DIM = 256
HEAD_DIM = 64
DIFF_HEADS = 4
DIFF_QK = 2 * HEAD_DIM
DIFF_V = 2 * HEAD_DIM
DIFF_WIDTH = DIFF_HEADS * DIFF_V
DIL_HEADS = 8
DIL_WIDTH = DIL_HEADS * HEAD_DIM
DIL_PATTERNS = ((128, 1), (512, 4), (2048, 16))
MIX_WIDTH = DIFF_WIDTH + DIL_WIDTH
Q_BLOCK = 128
NORM_EPS = 1e-6
MASK_VALUE = -1e30

IN_SPLIT_SIZES = (
    DIFF_HEADS * DIFF_QK,
    DIFF_HEADS * DIFF_QK,
    DIFF_WIDTH,
    DIL_WIDTH,
    DIL_WIDTH,
    DIL_WIDTH,
    MIX_WIDTH,
)
IN_WIDTH = sum(IN_SPLIT_SIZES)
IN_SPLIT_IDX = tuple(int(v) for v in np.cumsum(IN_SPLIT_SIZES)[:-1])


def rms_norm_2(t, g):
    tf = t.astype(jnp.float32)
    y = tf * lax.rsqrt(jnp.mean(tf * tf, axis=-1, keepdims=True) + NORM_EPS)
    return (y * g.astype(jnp.float32)).astype(t.dtype)

def alibi_slopes(n_heads):
    return jnp.exp2(-8.0 * jnp.arange(1, n_heads + 1, dtype=jnp.float32) / n_heads)

def diff_attention(q, k, v, lam, slopes):
    B, S, H, _, Dh = q.shape
    scale = Dh ** -0.5
    nqb = S // Q_BLOCK
    pos = jnp.arange(S)
    qb = q.reshape(B, nqb, Q_BLOCK, H, 2, Dh).transpose(1, 0, 2, 3, 4, 5)
    qpos = pos.reshape(nqb, Q_BLOCK)

    def block(args):
        qblk, qp = args
        s = jnp.einsum('bqhce,bkhce->bchqk', qblk, k).astype(jnp.float32) * scale
        dist = jnp.abs(qp[:, None] - pos[None, :]).astype(jnp.float32)
        s = s - slopes[:, None, None] * dist
        a = jax.nn.softmax(s, axis=-1)
        w = a[:, 0] - lam * a[:, 1]
        return jnp.einsum('bhqk,bkhe->bqhe', w.astype(v.dtype), v)

    out = lax.map(block, (qb, qpos))
    return out.transpose(1, 0, 2, 3, 4).reshape(B, S, H, 2 * Dh)

def dilated_branch(q, k, v, slopes, window, dilation):
    B, S, H, Dh = q.shape
    r = window // (2 * dilation)
    blk = r
    unit = dilation * blk
    Lp = -(-S // unit) * unit
    n = Lp // dilation
    nb = n // blk
    scale = Dh ** -0.5

    def split(t):
        t = jnp.pad(t, ((0, 0), (0, Lp - S), (0, 0), (0, 0)))
        return t.reshape(B, nb, blk, dilation, H, Dh)

    def window3(t):
        tp = jnp.pad(t, ((0, 0), (1, 1), (0, 0), (0, 0), (0, 0), (0, 0)))
        return jnp.concatenate([tp[:, :-2], tp[:, 1:-1], tp[:, 2:]], axis=2)

    qs = split(q)
    kw = window3(split(k))
    vw = window3(split(v))

    qi = jnp.arange(nb)[:, None] * blk + jnp.arange(blk)[None, :]
    kj = (jnp.arange(nb)[:, None] - 1) * blk + jnp.arange(3 * blk)[None, :]
    rel = qi[:, :, None] - kj[:, None, :]
    kpos = kj[:, :, None] * dilation + jnp.arange(dilation)[None, None, :]
    key_ok = ((kj >= 0)[:, :, None] & (kpos < S)).transpose(0, 2, 1)
    mask = (jnp.abs(rel) <= r)[:, None, None] & key_ok[:, :, None, None, :]
    dist = (dilation * jnp.abs(rel)).astype(jnp.float32)[:, None, None]
    bias = -slopes[:, None, None] * dist

    s = jnp.einsum('bnqche,bnkche->bnchqk', qs, kw).astype(jnp.float32) * scale + bias
    s = jnp.where(mask, s, MASK_VALUE)
    m = jnp.max(s, axis=-1, keepdims=True)
    e = jnp.exp(s - m)
    l = jnp.sum(e, axis=-1, keepdims=True)
    o = jnp.einsum('bnchqk,bnkche->bnqche', e.astype(v.dtype), vw)
    inv_l = (1.0 / l[..., 0]).transpose(0, 1, 4, 2, 3)[..., None]
    o = (o.astype(jnp.float32) * inv_l).reshape(B, Lp, H, Dh)[:, :S]
    lse = (m[..., 0] + jnp.log(l[..., 0])).transpose(0, 1, 4, 2, 3).reshape(B, Lp, H)[:, :S]
    return o, lse

def dilated_attention(q, k, v, slopes):
    outs, lses = [], []
    for window, dilation in DIL_PATTERNS:
        o, lse = dilated_branch(q, k, v, slopes, window, dilation)
        outs.append(o)
        lses.append(lse)
    w = jax.nn.softmax(jnp.stack(lses, axis=0), axis=0)
    out = jnp.sum(w[..., None] * jnp.stack(outs, axis=0), axis=0)
    return out.astype(q.dtype)

def second_inputs(seed: int = 0) -> dict:
    key = jax.random.key(seed)
    ks = jax.random.split(key, 20)
    f32 = jnp.float32

    def gain(k, n):
        return 1.0 + 0.02 * jax.random.normal(k, (DEPTH, n), f32)

    return {
        "x": jax.random.normal(ks[0], (BATCH, SEQ, D_MODEL), f32),
        "p": jax.random.normal(ks[1], (DEPTH, BATCH, SEQ, PLE_DIM), f32),
        "mix_norm_g": gain(ks[2], D_MODEL),
        "w_in": jax.random.normal(ks[3], (DEPTH, D_MODEL, IN_WIDTH), f32) * D_MODEL ** -0.5,
        "diff_q_norm_g": gain(ks[4], HEAD_DIM),
        "diff_k_norm_g": gain(ks[5], HEAD_DIM),
        "lambda_q1": 0.1 * jax.random.normal(ks[6], (DEPTH, HEAD_DIM), f32),
        "lambda_k1": 0.1 * jax.random.normal(ks[7], (DEPTH, HEAD_DIM), f32),
        "lambda_q2": 0.1 * jax.random.normal(ks[8], (DEPTH, HEAD_DIM), f32),
        "lambda_k2": 0.1 * jax.random.normal(ks[9], (DEPTH, HEAD_DIM), f32),
        "diff_sub_norm_g": gain(ks[10], DIFF_V),
        "dil_q_norm_g": gain(ks[11], HEAD_DIM),
        "dil_k_norm_g": gain(ks[12], HEAD_DIM),
        "w_out": jax.random.normal(ks[13], (DEPTH, MIX_WIDTH, D_MODEL), f32) * MIX_WIDTH ** -0.5,
        "ple_norm_g": gain(ks[14], D_MODEL),
        "w_ple_gate": jax.random.normal(ks[15], (DEPTH, D_MODEL, D_MODEL), f32) * D_MODEL ** -0.5,
        "w_ple_proj": jax.random.normal(ks[16], (DEPTH, PLE_DIM, D_MODEL), f32) * PLE_DIM ** -0.5,
    }

def second_block(x, p, mix_norm_g, w_in, diff_q_norm_g, diff_k_norm_g,
              lambda_q1, lambda_k1, lambda_q2, lambda_k2, diff_sub_norm_g,
              dil_q_norm_g, dil_k_norm_g, w_out, ple_norm_g, w_ple_gate, w_ple_proj):
    B, S, _ = x.shape
    diff_slopes = alibi_slopes(DIFF_HEADS)
    dil_slopes = alibi_slopes(DIL_HEADS)
    for i in range(DEPTH):
        lam_init = 0.8 - 0.6 * math.exp(-0.3 * i)
        h = rms_norm_2(x, mix_norm_g[i])
        u = h @ w_in[i]
        dq, dk, dv, bq, bk, bv, z = jnp.split(u, IN_SPLIT_IDX, axis=-1)

        dq = rms_norm_2(dq.reshape(B, S, DIFF_HEADS, 2, HEAD_DIM), diff_q_norm_g[i])
        dk = rms_norm_2(dk.reshape(B, S, DIFF_HEADS, 2, HEAD_DIM), diff_k_norm_g[i])
        dv = dv.reshape(B, S, DIFF_HEADS, DIFF_V)
        lam = (jnp.exp(jnp.sum(lambda_q1[i].astype(jnp.float32) * lambda_k1[i].astype(jnp.float32)))
               - jnp.exp(jnp.sum(lambda_q2[i].astype(jnp.float32) * lambda_k2[i].astype(jnp.float32)))
               + lam_init)
        a = diff_attention(dq, dk, dv, lam, diff_slopes)
        a = rms_norm_2(a, diff_sub_norm_g[i]) * (1.0 - lam_init)
        a = a.reshape(B, S, DIFF_WIDTH)

        bq = rms_norm_2(bq.reshape(B, S, DIL_HEADS, HEAD_DIM), dil_q_norm_g[i])
        bk = rms_norm_2(bk.reshape(B, S, DIL_HEADS, HEAD_DIM), dil_k_norm_g[i])
        bv = bv.reshape(B, S, DIL_HEADS, HEAD_DIM)
        b = dilated_attention(bq, bk, bv, dil_slopes).reshape(B, S, DIL_WIDTH)

        y = jnp.concatenate([a, b], axis=-1) * jax.nn.silu(z)
        x = x + y @ w_out[i]

        gate = jax.nn.sigmoid(rms_norm_2(x, ple_norm_g[i]) @ w_ple_gate[i])
        x = x + gate * (p[i] @ w_ple_proj[i])
    return x


def setup_inputs(seed=0):
    out = dict(first_inputs(seed))
    for name, value in second_inputs(seed + 1).items():
        if name != "x":
            out[name + "_2"] = value
    return out


def reference(
    x, c, w_ada, b_ada, g_norm_mix, w_in, b_gate, w_fourier, w_conv, w_conv_out, w_o,
    g_norm_moe, w_router, b_router, w_gate_e, w_up_e, w_down_e, g_final, p_2, mix_norm_g_2,
    w_in_2, diff_q_norm_g_2, diff_k_norm_g_2, lambda_q1_2, lambda_k1_2, lambda_q2_2,
    lambda_k2_2, diff_sub_norm_g_2, dil_q_norm_g_2, dil_k_norm_g_2, w_out_2, ple_norm_g_2,
    w_ple_gate_2, w_ple_proj_2,
):
    x = first_block(
        x, c, w_ada, b_ada, g_norm_mix, w_in, b_gate, w_fourier, w_conv, w_conv_out, w_o,
        g_norm_moe, w_router, b_router, w_gate_e, w_up_e, w_down_e, g_final,
    )
    return second_block(
        x, p_2, mix_norm_g_2, w_in_2, diff_q_norm_g_2, diff_k_norm_g_2, lambda_q1_2,
        lambda_k1_2, lambda_q2_2, lambda_k2_2, diff_sub_norm_g_2, dil_q_norm_g_2,
        dil_k_norm_g_2, w_out_2, ple_norm_g_2, w_ple_gate_2, w_ple_proj_2,
    )


_drawn_inputs = setup_inputs


def setup_inputs(seed=0):
    import zlib

    import numpy as np

    out = dict(_drawn_inputs(seed))
    spreads = {}
    factors = {'b_ada': 2.724,
     'g_norm_mix': 6.513,
     'b_gate': 8.0,
     'g_norm_moe': 8.0,
     'b_router': 8.0,
     'g_final': 2.761,
     'mix_norm_g_2': 4.783,
     'diff_q_norm_g_2': 8.0,
     'diff_k_norm_g_2': 8.0,
     'lambda_q1_2': 4.313,
     'lambda_k1_2': 3.138,
     'lambda_k2_2': 2.794,
     'diff_sub_norm_g_2': 8.0,
     'dil_q_norm_g_2': 8.0,
     'dil_k_norm_g_2': 8.0,
     'ple_norm_g_2': 8.0}
    for name, (base, spread) in spreads.items():
        noise = np.random.default_rng([zlib.crc32(name.encode()), seed]).standard_normal(out[name].shape)
        drawn = base * np.exp(spread * noise) if base else spread * noise
        out[name] = __import__('jax').numpy.asarray(drawn.astype(out[name].dtype))
    for name, factor in factors.items():
        out[name] = (out[name] * factor).astype(out[name].dtype)
    return out
```

```python
from contextlib import ExitStack

import numpy as np

import concourse.bass as bass
from concourse import mybir

F32 = mybir.dt.float32
ALU = mybir.AluOpType
ACT = mybir.ActivationFunctionType
AX = mybir.AxisListType

P = 128
SEQ, D = 256, 1024
TT = SEQ // P
KD = D // P
BANK = 512
DF = 512
FG = DF // P
NE, CAP, DE = 16, 32, 2048
SLOT = 2048
RING = 16
EPS = 1e-6
UNPICKED = 1000.0
LAM_INIT = 0.2
DH = 64
SCALE = DH ** -0.5

ADA0, WIN, ADA1, ADA2, WF, WCO, WO = 8, 22, 8, 8, 2, 4, 4
HEAD_SLOTS = ADA0 + WIN + ADA1 + ADA2 + WF + WCO + WO
EXPERT_SLOTS = 24
TAIL_RING = RING // 2
FIRST_TAIL = HEAD_SLOTS + NE * EXPERT_SLOTS

C_C, C_GMIX, C_GMOE, C_MIX2, C_PLE, C_BADA, C_BGATE, C_CONV = 0, 8, 16, 24, 32, 40, 88, 104
Q_SHIFT_M, Q_SCALE_M, Q_GATE_M, Q_SHIFT_F, Q_SCALE_F, Q_GATE_F = 0, 8, 16, 24, 32, 40


def shape_constants():
    s = np.arange(SEQ)
    a = 2 * np.pi * np.outer(s, s) / SEQ
    dft_seq = np.concatenate([np.cos(a), np.sin(a)], 1) / np.sqrt(SEQ)
    g = np.arange(P)
    b = 2 * np.pi * np.outer(g, g) / P
    dft_group = np.concatenate([np.cos(b), -np.sin(b)], 1) / np.sqrt(P)
    before = (g[:, None] < g[None, :]).astype(np.float32)
    slots = np.broadcast_to(np.arange(CAP) - UNPICKED, (P, CAP))
    small = np.concatenate([np.eye(P), before, slots], 1)
    dist = np.abs(s[:, None] - s[None, :])
    count = np.zeros((SEQ, SEQ))
    for window, dilation in ((128, 1), (512, 4), (2048, 16)):
        count += (dist % dilation == 0) & (dist // dilation <= window // (2 * dilation))
    log_count = np.where(count > 0, np.log(np.maximum(count, 1)), -1e30)
    diff = [-(2.0 ** (-8.0 * (h + 1) / 4)) * dist for h in range(4)]
    dil = [-(2.0 ** (-8.0 * (h + 1) / 8)) * dist + log_count for h in range(8)]
    bias = np.stack(diff + dil, 1)
    return {n: np.ascontiguousarray(v, dtype=np.float32) for n, v in
            dict(dft_seq=dft_seq, dft_group=dft_group, small=small, bias=bias).items()}

HEAD_UNITS = [("fourier_in", 2), ("v0", 2), ("seq01", 0), ("c0", 2), ("seq23", 0), ("b0", 2),
              ("group", 0), ("v1", 2), ("c1", 2), ("b1", 2), ("ga0", 2), ("ga1", 2), ("ya0", 0), ("ya1", WF),
              ("gb0", 2), ("gb1", 2), ("yb0", 0), ("yb1", WCO)]
MIX_UNIT = len(HEAD_UNITS)
TAIL_UNITS = [("q_diff", 2), ("k_diff", 2), ("q_dil", 2), ("turn_q_diff", 0), ("turn_k_diff", 0), ("k_dil", 2),
              ("turn_q_dil", 0), ("v_diff", 2), ("turn_k_dil", 0), ("v_dil", 2), ("turn_w0", 0), ("z0", 2),
              ("turn_w1", 0), ("pv_diff", 0), ("z1", 2), ("turn_e0a", 0), ("turn_e0b", 0), ("pv_dil0", 0),
              ("turn_cat0", 0), ("turn_e1a", 0), ("turn_e1b", 0), ("pv_dil1", 0), ("turn_cat1", 0)]
SCORES_AFTER = {"turn_k_diff": 0, "turn_k_dil": 1, "turn_w0": 2, "pv_diff": 3}
OUT_UNIT = len(TAIL_UNITS)
GATE_UNIT = OUT_UNIT + 2
ADA_BEFORE = {u: [divmod(n, KD)] for n, u in enumerate(list(range(1, 13)))}
ADA_BEFORE |= {14: [divmod(12, KD), divmod(13, KD)], 15: [divmod(14, KD)], 16: [divmod(15, KD)]}
ADA_BEFORE = {u: [(1 + b, k) for b, k in steps] for u, steps in ADA_BEFORE.items()}
IN_CHUNK = {"fourier_in": 0, "v0": 1, "v1": 2, "b0": 3, "b1": 4, "c0": 5, "c1": 6, "ga0": 7, "ga1": 8, "gb0": 9, "gb1": 10}
IN2_CHUNK = {"q_diff": 0, "k_diff": 1, "v_diff": 2, "q_dil": 3, "k_dil": 4, "v_dil": 5, "z0": 6, "z1": 7}


def build(nc, t, out):
    ctx = ExitStack()
    with ctx:
        def sem(name):
            return ctx.enter_context(nc.semaphore(name))

        ring = ctx.enter_context(nc.sbuf_tensor("ring", [P, RING, SLOT], F32))
        psum = ctx.enter_context(nc.psum_tensor("psum", [P, 8, BANK], F32))
        SIZE = 20400
        arena = ctx.enter_context(nc.sbuf_tensor("arena", [P, SIZE], F32))
        top = [0]

        def own(n):
            top[0] += n
            return arena[:, top[0] - n:top[0]]

        def shaped(ap, **dims):
            names = list(dims)
            return ap.rearrange(f"p ({' '.join(names)}) -> p {' '.join(names)}", **dims)

        x = shaped(own(TT * D), t=TT, d=D)
        xr_flat = own(TT * D)
        xr = shaped(xr_flat, t=TT, d=D)
        ht_flat = own(TT * D)
        ht = shaped(ht_flat, k=KD, s=SEQ)
        small = own(P + P + CAP)
        ident, before, slot_no = small[:, 0:P], small[:, P:2 * P], small[:, 2 * P:2 * P + CAP]
        ones = own(P)
        col = own(P)
        gain = own(8)
        sub_gain = own(1)
        c_act = own(KD)
        mod_t = own(48)
        mod_a = own(2 * KD)
        stat = shaped(own(5 * 4 * TT), n=5, c=4, t=TT)
        lam_in = shaped(own(4 * DH), v=4, d=DH)
        lam_s = own(8)
        soft = shaped(own(4 * 4 * 8), a=4, c=4, h=8)
        head_stat = shaped(own(4 * 16), c=4, h=16)
        cat_flat = own(2 * D)
        gm_row, gf_row = cat_flat[:, 0:D], cat_flat[:, D:2 * D]
        cat = shaped(cat_flat, t=TT, d=D)
        gfin = own(D)
        stage = top[0]

        def area(at, n):
            assert stage + at + n <= SIZE, stage + at + n - SIZE
            return arena[:, stage + at:stage + at + n]

        c_rep = shaped(area(0, 256), k=KD, r=32)
        dftg = area(256, 256)
        vt = shaped(area(512, 1024), k=4, s=SEQ)
        cv = shaped(area(1536, 4 * 258), k=4, s=258)
        conv = shaped(area(2568, 1024), k=4, s=SEQ)
        st = shaped(area(3592, 2048), k=KD, s=SEQ)
        ga = shaped(area(5640, 2048), k=KD, s=SEQ)
        gb = shaped(area(7688, 2048), k=KD, s=SEQ)
        vec1, vec2, sig_c = area(3592, P), area(9736, P), area(3848, KD)
        mod_rows = [area(5640, BANK), area(3592, BANK), area(4104, BANK)]
        dfts = shaped(gfin, t=TT, n=2 * SEQ)
        u_rows = shaped(gm_row, t=TT, d=DF)
        ab = shaped(xr_flat, g=FG, s=2 * SEQ)
        fm = shaped(gf_row, g=FG, s=SEQ)
        diag = [area(512, 1024), area(2568, 1024)]
        mix_tmp = shaped(area(1536, 2 * BANK), j=2, c=BANK)
        xet = shaped(area(0, KD * NE * CAP), k=KD, n=NE * CAP)
        cur = [shaped(area(4096 + 256 * h, 256), k=KD, s=CAP) for h in range(2)]
        gw_cur = [shaped(area(4608 + 256 * h, 256), t=TT, r=4, s=CAP) for h in range(2)]
        gwt = shaped(area(5120, 256), t=TT, m=P)
        sig_a = area(5376, BANK)
        act_h = area(5888, BANK)
        act_t = shaped(area(6400, BANK), c=4, m=P)
        y = shaped(area(6912, 2 * BANK), n=2, c=BANK)
        wr = shaped(area(7936, P), k=KD, e=NE)
        br = area(8064, NE)
        logit = shaped(area(8080, 32), t=TT, e=NE)
        prob = shaped(area(8112, 32), t=TT, e=NE)
        sel = shaped(area(8144, 32), t=TT, e=NE)
        slot_of = shaped(area(8176, 32), t=TT, e=NE)
        route = shaped(area(8208, 8), c=4, t=TT)
        prob_t = area(8216, SEQ)
        left_t = area(8472, SEQ)
        top8 = area(8728, 8)
        p_rows = shaped(area(8736, 512), t=TT, c=SEQ)
        zero = act_h
        pick = shaped(ht_flat[:, 0:1024], t=TT, e=NE, s=CAP)
        weigh = shaped(ht_flat[:, 1024:2048], t=TT, e=NE, s=CAP)
        weigh_flat = shaped(ht_flat[:, 1024:2048], t=TT, n=NE * CAP)
        pick_flat = shaped(ht_flat[:, 0:1024], t=TT, n=NE * CAP)
        spare = ring[:, 0:TAIL_RING, :].rearrange("p a b -> p (a b)")
        bias = shaped(spare[:, 0:6144], t=TT, h=12, s=SEQ)
        qz = [shaped(spare[:, 6144 + 2048 * i:8192 + 2048 * i], k=4, c=2, s=SEQ) for i in range(2)]
        kt = [shaped(spare[:, 10240 + 1024 * i:11264 + 1024 * i], k=4, s=SEQ) for i in range(2)]
        v = shaped(spare[:, 12288:14336], t=TT, d=D)
        szt = shaped(spare[:, 14336:16384], k=KD, s=SEQ)
        s0_flat, wt_flat = area(0, 2048), area(2048, 2048)
        scores = [shaped(f, h=8, s=SEQ) for f in (xr_flat, s0_flat)]
        qn = [shaped(f, t=TT, c=512) for f in
              (wt_flat[:, 0:1024], wt_flat[:, 1024:2048], s0_flat[:, 0:1024], s0_flat[:, 1024:2048])]
        wt = shaped(wt_flat, i=16, m=P)
        pp = shaped(area(4096, 2048), t=TT, d=D)
        sqt = shaped(area(6144, 1024), t=TT, c=512)
        sgz = shaped(area(7168, 1024), k=4, s=SEQ)
        pt = shaped(area(8192, 512), c=2, s=SEQ)
        gt = shaped(s0_flat, t=TT, d=D)

        def bank(b, **dims):
            return shaped(psum[:, b, :], **dims) if dims else psum[:, b, :]

        x_loaded, tables_loaded, vec_loaded, lam_loaded = (sem(n) for n in ("x_loaded", "tables_loaded", "vec_loaded", "lam_loaded"))
        gain_loaded, gain_turned, gain_ready = sem("gain_loaded"), sem("gain_turned"), sem("gain_ready")
        dft_loaded, side_loaded, bias_loaded = (sem(n) for n in ("dft_loaded", "side_loaded", "bias_loaded"))
        loaded = [sem(f"slot{p}_loaded") for p in range(RING)]
        slot_used = sem("slot_used")
        memset_done = sem("memset_done")
        vec_turned, vec_ready = sem("vec_turned"), sem("vec_ready")
        sig_c_ready, c_ready = sem("sig_c_ready"), sem("c_ready")
        mod_rows_ready, mod_turned, mod_ready = sem("mod_rows_ready"), sem("mod_turned"), sem("mod_ready")
        diag_ready, gate_row_done, gate_row_ready = sem("diag_ready"), sem("gate_row_done"), sem("gate_row_ready")
        squared, mean_ready, root_ready, xr_ready = (sem(n) for n in ("squared", "mean_ready", "root_ready", "xr_ready"))
        norm_turned, norm_act, norm_dve = sem("norm_turned"), sem("norm_act"), sem("norm_dve")
        x_ready = sem("x_ready")
        first_ready, second_ready = sem("first_ready"), sem("second_ready")
        free = [sem(f"head_bank{b}_read") for b in range(4)]
        tfree = [sem(f"tail_bank{b}_read") for b in range(4)]
        dve_chain, act_chain, pool_chain = sem("dve_chain"), sem("act_chain"), sem("pool_chain")
        logits_done, exp_ready, prob_ready, prob_turned = (sem(n) for n in ("logits_done", "exp_ready", "prob_ready", "prob_turned"))
        soft_in = sem("soft_in")
        mask_ready, mask_turned, sel_ready, slots_done, pick_ready = (sem(n) for n in ("mask_ready", "mask_turned", "sel_ready", "slots_done", "pick_ready"))
        gathered, xet_act, xet_dve = sem("gathered"), sem("xet_act"), sem("xet_dve")
        cur_ready, gw_turned, gwt_ready = sem("cur_ready"), sem("gw_turned"), sem("gwt_ready")
        sig_ready, gated, act_ready, act_turned, act_t_ready = (sem(n) for n in ("sig_ready", "gated", "act_ready", "act_turned", "act_t_ready"))
        y_act, y_dve, scattered = sem("y_act"), sem("y_dve"), sem("scattered")
        pt_turned, pt_ready = sem("pt_turned"), sem("pt_ready")
        lam_sums, lam_exps, lam_ready = sem("lam_sums"), sem("lam_exps"), sem("lam_ready")
        qk_squared, qk_mean, qk_root, qn_ready = (sem(n) for n in ("qk_squared", "qk_mean", "qk_root", "qn_ready"))
        scores_done, scores_read, max_ready, exps_done, w_ready = (sem(n) for n in ("scores_done", "scores_read", "max_ready", "exps_done", "w_ready"))
        sgz_ready, cat_ready, yt_ready = sem("sgz_ready"), sem("cat_ready"), sem("yt_ready")
        gate_sig, out_ready, stored = sem("gate_sig"), sem("out_ready"), sem("stored")

        def rows_of(w, cols, k0, nk):
            return w[k0 * P:(k0 + nk) * P, cols[0]:cols[1]].rearrange("(k p) n -> p k n", p=P)

        def pair(w, chunk):
            return [rows_of(w, (chunk * 512, chunk * 512 + 512), 4 * half, 4) for half in range(2)]

        w_ada, w_in, w_in2 = t["w_ada"][0], t["w_in"][0], t["w_in_2"][0]
        ada = [[rows_of(w_ada, (b * SLOT, (b + 1) * SLOT), k, 1) for k in range(KD)] for b in range(3)]
        head_stream = list(ada[0])
        first_slot = {f"ada0_{k}": k for k in range(KD)}
        for u, (name, _) in enumerate(HEAD_UNITS):
            for b, k in ADA_BEFORE.get(u, ()):
                first_slot[f"ada{b}_{k}"] = len(head_stream)
                head_stream.append(ada[b][k])
            first_slot[name] = len(head_stream)
            if name in IN_CHUNK:
                head_stream += pair(w_in, IN_CHUNK[name])
            elif name == "ya0":
                head_stream += [rows_of(t["w_fourier"][0], (0, D), 2 * i, 2) for i in range(WF)]
            elif name == "yb0":
                head_stream += [rows_of(t["w_conv_out"][0], (0, D), 2 * i, 2) for i in range(WCO)]
        first_slot["w_o"] = len(head_stream)
        head_stream += [rows_of(t["w_o"][0], (0, D), 2 * i, 2) for i in range(WO)]
        assert len(head_stream) == HEAD_SLOTS
        tail_stream = [rows_of(t["w_ple_proj_2"][0], (0, D), 0, 2)]
        first_slot["w_pp"] = FIRST_TAIL
        for name, _ in TAIL_UNITS:
            if name in IN2_CHUNK:
                first_slot[name] = FIRST_TAIL + len(tail_stream)
                tail_stream += pair(w_in2, IN2_CHUNK[name])
        for name, w in (("w_out", "w_out_2"), ("w_gate", "w_ple_gate_2")):
            first_slot[name] = FIRST_TAIL + len(tail_stream)
            tail_stream += [rows_of(t[w][0], (0, D), 2 * i, 2) for i in range(4)]

        def place(s):
            if s < FIRST_TAIL:
                return s % RING, s // RING + 1
            p = RING - TAIL_RING + (s - FIRST_TAIL) % TAIL_RING
            return p, (FIRST_TAIL - 1 - p) // RING + 1 + (s - FIRST_TAIL) // TAIL_RING + 1

        def slot_in(s, **dims):
            return shaped(ring[:, place(s)[0], :], **dims)

        def arrived(eng, s):
            p, n = place(s)
            eng.wait_ge(loaded[p], 16 * n)

        ready_at = {}
        counts = {"first": 0, "second": 0}

        def plan(units, tag):
            for u, (name, slots) in enumerate(units):
                counts["first"] += 1
                ready_at[tag, u, 0] = (first_ready, counts["first"])
                if slots:
                    start = first_slot[name if name not in ("ya1", "yb1") else name[:2] + "0"]
                    ready_at[tag, u, 1] = (slot_used, start + slots)
                else:
                    counts["second"] += 1
                    ready_at[tag, u, 1] = (second_ready, counts["second"])

        plan(HEAD_UNITS, "head")
        plan(TAIL_UNITS, "tail")

        def await_bank(eng, tag, u, j):
            s, n = ready_at[tag, u, j]
            eng.wait_ge(s, n)

        def await_read(eng, sems, u):
            for j in range(2):
                eng.wait_ge(sems[2 * (u % 2) + j], u // 2 + 2)

        head_u = {name: u for u, (name, _) in enumerate(HEAD_UNITS)}
        tail_u = {name: u for u, (name, _) in enumerate(TAIL_UNITS)}
        block = ctx.enter_context(nc.Block())

        @block.sync
        def _(sp):
            sp.dma_start(x, t["x"][0].rearrange("(t p) d -> p t d", p=P)).then_inc(x_loaded, 16)
            for s, src in enumerate(head_stream):
                if s == 2:
                    sp.wait_ge(vec_loaded, 16 * VEC_DMAS)
                if s >= RING:
                    sp.wait_ge(slot_used, s - RING + 1)
                sp.dma_start(slot_in(s, k=src.shape[1], n=src.shape[2]), src).then_inc(loaded[s % RING], 16)
            with sp.Fori(0, NE // 2) as i:
                for h in range(2):
                    for j in range(EXPERT_SLOTS):
                        s = HEAD_SLOTS + h * EXPERT_SLOTS + j
                        w = t[("w_gate_e", "w_up_e", "w_down_e")[j // 8]][0]
                        w = w[bass.ds(2 * i + h, 1)]
                        if j < 16:
                            src = w[:, (j % 8) * P:(j % 8 + 1) * P, :].rearrange("e (k p) n -> p (e k) n", p=P)
                        else:
                            src = w[:, (j - 16) * 2 * P:(j - 15) * 2 * P, :].rearrange("e (k p) n -> p (e k) n", p=P)
                        sp.wait_ge(slot_used, 2 * EXPERT_SLOTS * i + (s - RING + 1))
                        sp.dma_start(slot_in(s, k=src.shape[1], n=src.shape[2]), src).then_inc(loaded[s % RING], 16)
            for n, src in enumerate(tail_stream):
                s = FIRST_TAIL + n
                sp.wait_ge(slot_used, s - RING + 1 if n < TAIL_RING else s - TAIL_RING + 1)
                sp.dma_start(slot_in(s, k=src.shape[1], n=src.shape[2]), src).then_inc(loaded[place(s)[0]], 16)
            for tt in range(TT):
                sp.wait_ge(out_ready, 2 * tt + 2)
                sp.dma_start(out[0, tt * P:(tt + 1) * P, :], x[:, tt, :]).then_inc(stored, 16)
            sp.wait_ge(stored, 16 * TT)

        @block.gpsimd
        def _(pool):
            nc.gpsimd.memset(ones, 1.0).then_inc(memset_done, 1)
            nc.gpsimd.memset(cv[:, :, 0:1], 0.0).then_inc(memset_done, 1)
            nc.gpsimd.memset(cv[:, :, 257:258], 0.0).then_inc(memset_done, 1)
            pool.dma_start(dfts, t["dft_seq"].rearrange("(t p) n -> p t n", p=P)).then_inc(dft_loaded, 16)
            pool.dma_start(dftg, t["dft_group"]).then_inc(dft_loaded, 16)
            for row, name in enumerate(("diff_q_norm_g_2", "diff_k_norm_g_2", "dil_q_norm_g_2", "dil_k_norm_g_2")):
                for half in range(2):
                    pool.dma_start(vec2[row:row + 1, half * DH:(half + 1) * DH], t[name]).then_inc(gain_loaded, 16)
            pool.dma_start(vec2[4:5, :], t["diff_sub_norm_g_2"]).then_inc(gain_loaded, 16)
            for n, name in enumerate(("lambda_q1_2", "lambda_k1_2", "lambda_q2_2", "lambda_k2_2")):
                pool.dma_start(lam_in[:, n, :], t[name][0].partition_broadcast(P)).then_inc(lam_loaded, 16)
            await_bank(pool, "head", head_u["seq23"], 1)
            pool.dma_start(gfin, t["g_final"].partition_broadcast(P)).then_inc(side_loaded, 16)
            pool.wait_ge(slot_used, first_slot["w_o"] + 1)
            with nc.allow_non_contiguous_dma(reason="64 B rows of the small router"):
                pool.dma_start(wr, t["w_router"][0].rearrange("(k p) e -> p k e", p=P)).then_inc(side_loaded, 16)
            pool.dma_start(br, t["b_router"][0].partition_broadcast(P)).then_inc(side_loaded, 16)
            pool.dma_start(p_rows, t["p_2"][0, 0].rearrange("(t p) c -> p t c", p=P)).then_inc(side_loaded, 16)

            def take(e, h):
                nc.gpsimd.tensor_copy(cur[h], xet[:, :, bass.ds(e * CAP, CAP)]).then_inc(cur_ready, 1)
                for tt in range(TT):
                    src = weigh_flat[:, tt, bass.ds(e * CAP, CAP)].unsqueeze(1).broadcast_to([P, 4, CAP])
                    nc.gpsimd.tensor_copy(gw_cur[h][:, tt], src).then_inc(cur_ready, 1)

            pool.wait_ge(xet_act, 4)
            pool.wait_ge(xet_dve, 4)
            pool.wait_ge(pick_ready, 4)
            take(0, 0)
            take(1, 1)
            with pool.Fori(0, NE // 2 - 1) as i:
                for h in range(2):
                    pool.wait_ge(slot_used, 2 * EXPERT_SLOTS * i + (HEAD_SLOTS + h * EXPERT_SLOTS + 16))
                    take(2 * i + (2 + h), h)
            pool.wait_ge(slot_used, FIRST_TAIL)
            pool.dma_start(bias, t["bias"].rearrange("(t p) h s -> p t h s", p=P)).then_inc(bias_loaded, 16)
            for i in range(2):
                nc.gpsimd.memset(qz[i][DH:P, :, 0, :], 0.0).then_inc(memset_done, 1)
                nc.gpsimd.memset(qz[i][0:DH, :, 1, :], 0.0).then_inc(memset_done, 1)

        @block.tensor
        def _(pe):
            mm = nc.tensor.matmul

            def end_first(ins):
                ins.then_inc(first_ready, 1)

            def end_second(ins, slots):
                if slots:
                    ins.then_inc(slot_used, slots)
                else:
                    ins.then_inc(second_ready, 1)

            def transposed_product(w, nk, rhs, u, slots, tile0=0):
                for j in range(2):
                    for c in range(2):
                        for k in range(nk):
                            last = mm(bank(2 * (u % 2) + j, c=2, s=SEQ)[:, c, :], w(k, tile0 + 2 * j + c), rhs[:, k, :],
                                      start=(k == 0), stop=(k == nk - 1))
                    end_first(last) if j == 0 else end_second(last, slots)

            def rows_product(w, u, slots):
                for tt in range(TT):
                    for k in range(KD):
                        last = mm(bank(2 * (u % 2) + tt), ht[:, k, tt * P:(tt + 1) * P], w(k), start=(k == 0), stop=(k == KD - 1))
                    end_first(last) if tt == 0 else end_second(last, slots)

            def pair_weight(name):
                s = first_slot[name]
                arrived(pe, s)
                arrived(pe, s + 1)
                halves = [slot_in(s + i, k=4, n=512) for i in range(2)]
                return (lambda k, c: halves[k // 4][:, k % 4, c * P:(c + 1) * P]), (lambda k: halves[k // 4][:, k % 4, :])

            def wide_weight(s, n):
                for i in range(n):
                    arrived(pe, s + i)
                return lambda k, c: slot_in(s + k // 2, k=2, n=D)[:, k % 2, c * P:(c + 1) * P]

            def wide_rows(s, u, lhs):
                for i in range(4):
                    arrived(pe, s + i)
                    w = slot_in(s + i, k=2, n=D)
                    for kk in range(2):
                        k = 2 * i + kk
                        for tt in range(TT):
                            for n in range(2):
                                last = mm(bank(2 * ((u + tt) % 2) + n), lhs[:, k, tt * P:(tt + 1) * P], w[:, kk, n * BANK:(n + 1) * BANK],
                                          start=(k == 0), stop=(k == KD - 1))
                    last.then_inc(slot_used, 1)

            def begin(sems, u):
                for j in range(2):
                    pe.wait_ge(sems[2 * (u % 2) + j], u // 2 + 1)

            def turn_norm(n, first_bank):
                pe.wait_ge(xr_ready, 2 * n + 2)
                for q in range(4):
                    for c in range(2):
                        for tt in range(TT):
                            last = nc.tensor.transpose(bank(first_bank + q, c=2, t=TT, m=P)[:, c, tt, :],
                                                       xr[:, tt, (2 * q + c) * P:(2 * q + c + 1) * P], ident)
                    last.then_inc(norm_turned, 1)

            def modulation(b, k, to):
                s = first_slot[f"ada{b}_{k}"]
                arrived(pe, s)
                for g in range(4):
                    last = mm(psum[32 * g:32 * g + 32, to, :], c_rep[:, k, :], slot_in(s, g=4, n=512)[:, g, :],
                              start=(k == 0), stop=(k == KD - 1), tile_position=(0, 32 * g))
                last.then_inc(slot_used, 1)

            def turn_modulation(b, to):
                pe.wait_ge(mod_rows_ready, b + 1)
                for c in range(4):
                    last = nc.tensor.transpose(bank(to, c=4, m=P)[:, c, :], mod_rows[b][:, c * P:(c + 1) * P], ident)
                last.then_inc(mod_turned, 1)

            pe.wait_ge(tables_loaded, 16)
            pe.wait_ge(vec_loaded, 16 * VEC_DMAS)
            nc.tensor.transpose(psum[:, 7, 0:P], vec1, ident).then_inc(vec_turned, 1)
            turn_norm(0, 0)
            pe.wait_ge(c_ready, 1)
            for k in range(KD):
                modulation(0, k, 4)
            turn_modulation(0, 5)

            for u, (name, slots) in enumerate(HEAD_UNITS):
                for bk in ADA_BEFORE.get(u, ()):
                    if bk == (1, 0):
                        pe.wait_ge(mod_ready, 1)
                    modulation(*bk, 3 + bk[0])
                if name == "fourier_in":
                    for b in range(4):
                        pe.wait_ge(free[b], 1)
                    rows_product(pair_weight(name)[1], u, slots)
                    continue
                begin(free, u)
                if name in IN_CHUNK:
                    transposed_product(pair_weight(name)[0], KD, ht, u, slots)
                elif name in ("seq01", "seq23"):
                    if name == "seq01":
                        pe.wait_ge(dft_loaded, 32)
                        await_read(pe, free, head_u["fourier_in"])
                    for j in range(2):
                        g = 2 * (name == "seq23") + j
                        for tt in range(TT):
                            last = mm(bank(2 * (u % 2) + j), u_rows[:, tt, g * P:(g + 1) * P], dfts[:, tt, :], start=(tt == 0), stop=(tt == 1))
                        end_first(last) if j == 0 else end_second(last, 0)
                elif name == "group":
                    await_read(pe, free, head_u["seq23"])
                    for j in range(2):
                        for c in range(2):
                            for part in range(2):
                                last = mm(bank(2 * (u % 2) + j, c=2, s=SEQ)[:, c, :], dftg[:, part * P:(part + 1) * P],
                                          ab[:, 2 * j + c, part * SEQ:(part + 1) * SEQ], start=(part == 0), stop=(part == 1))
                        end_first(last) if j == 0 else end_second(last, 0)
                elif name in ("ya0", "ya1"):
                    await_read(pe, free, head_u["group"])
                    transposed_product(wide_weight(first_slot["ya0"], WF), FG, fm, u, slots, 4 * int(name[2]))
                else:
                    await_read(pe, free, head_u["b1"])
                    transposed_product(wide_weight(first_slot["yb0"], WCO), KD, st, u, slots, 4 * int(name[2]))
            pe.wait_ge(gain_loaded, 144)
            nc.tensor.transpose(psum[:, 6, 0:5], vec2[0:5, :], ident[0:5, 0:5]).then_inc(gain_turned, 1)
            pe.wait_ge(gain_ready, 1)
            turn_modulation(1, 6)
            turn_modulation(2, 7)
            for g in range(2):
                pe.wait_ge(diag_ready, g + 1)
                pe.wait_ge(mod_rows_ready, 3)
                for n in range(2):
                    last = mm(bank(4 + 2 * g + n), ones, diag[g][:, n * BANK:(n + 1) * BANK], start=True, stop=True)
                last.then_inc(gate_row_done, 1)
            begin(free, MIX_UNIT)
            begin(free, MIX_UNIT + 1)
            wide_rows(first_slot["w_o"], MIX_UNIT, ga)

            pe.wait_ge(gate_row_ready, 4)
            turn_norm(1, 4)
            pe.wait_ge(side_loaded, 64)
            pe.wait_ge(norm_act, 2)
            pe.wait_ge(norm_dve, 2)
            await_read(pe, free, MIX_UNIT)
            await_read(pe, free, MIX_UNIT + 1)
            for tt in range(TT):
                for k in range(KD):
                    last = mm(psum[:, 0, tt * NE:(tt + 1) * NE], ht[:, k, tt * P:(tt + 1) * P], wr[:, k, :], start=(k == 0), stop=(k == KD - 1))
            last.then_inc(logits_done, 1)
            pe.wait_ge(prob_ready, 1)
            for tt in range(TT):
                last = nc.tensor.transpose(psum[0:NE, 1, tt * P:(tt + 1) * P], prob[:, tt, :], ident)
            last.then_inc(prob_turned, 1)
            pe.wait_ge(mask_ready, 1)
            for tt in range(TT):
                last = nc.tensor.transpose(psum[:, 2, tt * NE:(tt + 1) * NE], left_t[0:NE, tt * P:(tt + 1) * P], ident[0:NE, 0:NE])
            last.then_inc(mask_turned, 1)
            pe.wait_ge(sel_ready, 1)
            mm(psum[:, 3, 0:NE], before, sel[:, 0, :], start=True, stop=True)
            mm(psum[:, 3, NE:2 * NE], ones, sel[:, 0, :], start=True, stop=False)
            mm(psum[:, 3, NE:2 * NE], before, sel[:, 1, :], start=False, stop=True).then_inc(slots_done, 1)
            pe.wait_ge(pick_ready, 2)
            for k in range(KD):
                if k >= 4:
                    pe.wait_ge(xet_act if k % 2 == 0 else xet_dve, (k - 4) // 2 + 1)
                for tt in range(TT):
                    last = mm(bank(4 + k % 4), xr[:, tt, k * P:(k + 1) * P], pick_flat[:, tt, :], start=(tt == 0), stop=(tt == 1))
                last.then_inc(gathered, 1)
            pe.wait_ge(xet_act, 4)
            pe.wait_ge(xet_dve, 4)
            for b in range(4):
                mm(bank(4 + b), zero[:, 0:P], zero, start=True, stop=True)

            with pe.Fori(0, NE // 2) as i:
                for h in range(2):
                    def slot_wait(j):
                        s = HEAD_SLOTS + h * EXPERT_SLOTS + j
                        pe.wait_ge(loaded[s % RING], 48 * i + 16 * (s // RING + 1))
                        return s
                    pe.wait_ge(cur_ready, 6 * i + 3 * (h + 1))
                    for tt in range(TT):
                        last = nc.tensor.transpose(bank(2, t=4, m=P)[:, tt, :], gw_cur[h][:, tt].rearrange("p r s -> p (r s)"), ident)
                    last.then_inc(gw_turned, 1)
                    for b in range(2):
                        for k in range(KD):
                            s = slot_wait(8 * b + k)
                            for g in range(4):
                                last = mm(psum[32 * g:32 * g + 32, b, :], cur[h][:, k, :], slot_in(s, g=4, n=512)[:, g, :],
                                          start=(k == 0), stop=(k == KD - 1), tile_position=(0, 32 * g))
                            last.then_inc(slot_used, 1)
                    pe.wait_ge(act_ready, 2 * i + (h + 1))
                    for c in range(4):
                        last = nc.tensor.transpose(bank(0, c=4, m=P)[:, c, :], act_h[:, c * P:(c + 1) * P], ident)
                    last.then_inc(act_turned, 1)
                    pe.wait_ge(act_t_ready, 2 * i + (h + 1))
                    pe.wait_ge(gwt_ready, 2 * i + (h + 1))
                    for j in range(8):
                        s = slot_wait(16 + j)
                        w = slot_in(s, k=2, n=D)
                        for n in range(2):
                            for kk in range(2):
                                f = 2 * j + kk
                                q = f % 4
                                last = mm(psum[32 * q:32 * q + 32, 2 + n, :], act_t[:, f % 4, (f // 4) * CAP:(f // 4 + 1) * CAP],
                                          w[:, kk, n * BANK:(n + 1) * BANK], start=(f < 4), stop=(f >= 12), tile_position=(0, 32 * q))
                        last.then_inc(slot_used, 1)
                    pe.wait_ge(y_act, 2 * i + (h + 1))
                    pe.wait_ge(y_dve, 2 * i + (h + 1))
                    for tt in range(TT):
                        for n in range(2):
                            last = mm(bank(4 + 2 * tt + n), gwt[:, tt, :], y[:, n, :], start=False, stop=True, skip_group_check=True)
                    last.then_inc(scattered, 1)

            for c in range(2):
                for tt in range(TT):
                    last = nc.tensor.transpose(bank(3, c=2, t=TT, m=P)[:, c, tt, :], p_rows[:, tt, c * P:(c + 1) * P], ident)
            last.then_inc(pt_turned, 1)
            pe.wait_ge(pt_ready, 1)
            arrived(pe, first_slot["w_pp"])
            w = slot_in(first_slot["w_pp"], k=2, n=D)
            for tt in range(TT):
                for n in range(2):
                    for k in range(2):
                        last = mm(bank(2 * tt + n), pt[:, k, tt * P:(tt + 1) * P], w[:, k, n * BANK:(n + 1) * BANK], start=(k == 0), stop=(k == 1))
            last.then_inc(slot_used, 1)
            turn_norm(2, 4)
            pe.wait_ge(norm_act, 4)
            pe.wait_ge(norm_dve, 4)

            def score_product(a):
                kind = ("diff", "dil")[a // 2]
                await_read(pe, tfree, tail_u["turn_q_" + kind])
                await_read(pe, tfree, tail_u["turn_k_" + kind])
                if a:
                    pe.wait_ge(scores_read, 4 * a)
                q, k = qz[a // 2], kt[a // 2]
                for j in range(4):
                    for c in range(2):
                        last = mm(bank(4 + j, c=2, s=SEQ)[:, c, :], q[:, j, c, (a % 2) * P:(a % 2 + 1) * P], k[:, j, :], start=True, stop=True)
                    last.then_inc(scores_done, 1)

            for u, (name, slots) in enumerate(TAIL_UNITS):
                begin(tfree, u)
                if name in ("z0", "z1"):
                    transposed_product(pair_weight(name)[0], KD, ht, u, slots)
                elif name in IN2_CHUNK:
                    rows_product(pair_weight(name)[1], u, slots)
                elif name.startswith(("turn_q", "turn_k")):
                    i = ("turn_q_diff", "turn_k_diff", "turn_q_dil", "turn_k_dil").index(name)
                    pe.wait_ge(qn_ready, 2 * i + 2)
                    for j in range(2):
                        for c in range(2):
                            for tt in range(TT):
                                last = nc.tensor.transpose(bank(2 * (u % 2) + j, c=2, t=TT, m=P)[:, c, tt, :],
                                                           qn[i][:, tt, (2 * j + c) * P:(2 * j + c + 1) * P], ident)
                        end_first(last) if j == 0 else end_second(last, 0)
                elif name.startswith("turn_w"):
                    a = int(name[6])
                    pe.wait_ge(w_ready, a + 1)
                    for j in range(2):
                        for c in range(2):
                            for kk in range(TT):
                                last = nc.tensor.transpose(bank(2 * (u % 2) + j, c=2, t=TT, m=P)[:, c, kk, :],
                                                           scores[a][:, 2 * (2 * j + c), kk * P:(kk + 1) * P], ident)
                        end_first(last) if j == 0 else end_second(last, 0)
                elif name.startswith("turn_e"):
                    a, part = int(name[6]), "ab".index(name[7])
                    pe.wait_ge(exps_done, 3 + a)
                    for j in range(2):
                        for c in range(2):
                            for kk in range(TT):
                                last = nc.tensor.transpose(bank(2 * (u % 2) + j, c=2, t=TT, m=P)[:, c, kk, :],
                                                           scores[a][:, 4 * part + 2 * j + c, kk * P:(kk + 1) * P], ident)
                        end_first(last) if j == 0 else end_second(last, 0)
                elif name == "pv_diff":
                    await_read(pe, tfree, tail_u["turn_w0"])
                    await_read(pe, tfree, tail_u["turn_w1"])
                    for tt in range(TT):
                        for hh in range(4):
                            for kk in range(TT):
                                last = mm(psum[:, 2 * (u % 2) + tt, hh * P:(hh + 1) * P], wt[:, 8 * tt + 2 * hh + kk, :], v[:, kk, hh * P:(hh + 1) * P],
                                          start=(kk == 0), stop=(kk == 1))
                        end_first(last) if tt == 0 else end_second(last, 0)
                elif name.startswith("pv_dil"):
                    await_read(pe, tfree, u - 2)
                    await_read(pe, tfree, u - 1)
                    for j in range(2):
                        for c in range(4):
                            hh = 4 * j + c
                            for kk in range(TT):
                                last = mm(psum[:, 2 * (u % 2) + j, c * DH:(c + 1) * DH], wt[:, 2 * hh + kk, :],
                                          v[:, kk, 512 + hh * DH:512 + (hh + 1) * DH], start=(kk == 0), stop=(kk == 1))
                        end_first(last) if j == 0 else end_second(last, 0)
                else:
                    i = int(name[-1])
                    if i == 0:
                        pe.wait_ge(cat_ready, 2)
                    else:
                        await_read(pe, tfree, tail_u["pv_dil0"])
                        await_read(pe, tfree, tail_u["pv_dil1"])
                    for j in range(2):
                        for c in range(2):
                            for tt in range(TT):
                                last = nc.tensor.transpose(bank(2 * (u % 2) + j, c=2, t=TT, m=P)[:, c, tt, :],
                                                           cat[:, tt, (4 * i + 2 * j + c) * P:(4 * i + 2 * j + c + 1) * P], ident)
                        end_first(last) if j == 0 else end_second(last, 0)
                if name in SCORES_AFTER:
                    score_product(SCORES_AFTER[name])
            begin(tfree, OUT_UNIT)
            begin(tfree, OUT_UNIT + 1)
            wide_rows(first_slot["w_out"], OUT_UNIT, ht)
            turn_norm(3, 4)
            pe.wait_ge(norm_act, 6)
            pe.wait_ge(norm_dve, 6)
            begin(tfree, GATE_UNIT)
            begin(tfree, GATE_UNIT + 1)
            wide_rows(first_slot["w_gate"], GATE_UNIT, ht)

        @block.scalar
        def _(act):
            f = nc.scalar.activation
            count = [0]

            def link(ins):
                count[0] += 1
                ins.then_inc(act_chain, 1)
                act.wait_ge(act_chain, count[0])

            act.dma_start(small, t["small"]).then_inc(tables_loaded, 16)
            for at, src in vec_sources(t):
                act.dma_start(vec1[at:at + src.shape[0], :], src).then_inc(vec_loaded, 16)

            def squares(n, wait):
                for tt in range(TT):
                    wait(tt)
                    f(xr[:, tt, :], x[:, tt, :], ACT.Square, accum_out=stat[:, n, 0, tt:tt + 1]).then_inc(squared, 1)

            def roots(n):
                act.wait_ge(mean_ready, n + 1)
                f(stat[:, n, 2, :], stat[:, n, 1, :], ACT.Sqrt).then_inc(root_ready, 1)

            def spread_norm(n, first_bank, scale, shift, sems=None):
                for q in (0, 2):
                    act.wait_ge(norm_turned, 4 * n + q + 1)
                    for c in range(2):
                        k = 2 * q + c
                        src = bank(first_bank + q, c=2, s=SEQ)[:, c, :]
                        if shift is None:
                            ins = f(ht[:, k, :], src, ACT.Copy, scale=scale[:, k:k + 1])
                        else:
                            ins = f(ht[:, k, :], src, ACT.Identity, scale=scale[:, k:k + 1], bias=shift[:, k:k + 1])
                    ins.then_inc(sems[q] if sems else norm_act, 1)

            squares(0, lambda tt: act.wait_ge(x_loaded, 16))
            roots(0)
            act.wait_ge(vec_ready, 1)
            f(sig_c, col[:, C_C:C_C + KD], ACT.Sigmoid).then_inc(sig_c_ready, 1)

            def modulation_rows(b, from_bank):
                act.wait_ge(slot_used, first_slot[f"ada{b}_{KD - 1}"] + 1)
                f(mod_rows[b], bank(from_bank), ACT.Copy).then_inc(mod_rows_ready, 1)

            modulation_rows(0, 4)
            act.wait_ge(mod_ready, 1)
            spread_norm(0, 0, mod_a[:, 0:KD], mod_t[:, Q_SHIFT_M:], free)

            for u, (name, _) in enumerate(HEAD_UNITS):
                b = 2 * (u % 2)
                if name == "fourier_in":
                    await_bank(act, "head", u, 0)
                    f(u_rows[:, 0, :], bank(b), ACT.Copy).then_inc(free[b], 1)
                elif name in ("v0", "v1"):
                    await_bank(act, "head", u, 0)
                    f(vt[:, 0:2, :], bank(b, c=2, s=SEQ), ACT.Copy).then_inc(free[b], 1)
                elif name in ("seq01", "seq23"):
                    await_bank(act, "head", u, 0)
                    f(ab[:, 2 * (name == "seq23"), :], bank(b), ACT.Copy).then_inc(free[b], 1)
                elif name == "group":
                    await_bank(act, "head", u, 0)
                    f(fm[:, 0:2, :], bank(b, c=2, s=SEQ), ACT.Copy).then_inc(free[b], 1)
                elif name[:2] in ("ga", "gb"):
                    gate, first = (ga, 0) if name[:2] == "ga" else (gb, KD)
                    for j in range(2):
                        await_bank(act, "head", u, j)
                        for c in range(2):
                            k = 4 * int(name[2]) + 2 * j + c
                            at = C_BGATE + first + k
                            ins = f(gate[:, k, :], bank(b + j, c=2, s=SEQ)[:, c, :], ACT.Sigmoid, bias=col[:, at:at + 1])
                        ins.then_inc(free[b + j], 1)
            await_bank(act, "head", head_u["yb1"], 1)
            modulation_rows(1, 4)
            modulation_rows(2, 5)
            for g, row in ((0, gm_row), (1, gf_row)):
                act.wait_ge(gate_row_done, g + 1)
                for n in range(2):
                    f(row[:, n * BANK:(n + 1) * BANK], bank(4 + 2 * g + n), ACT.Copy).then_inc(gate_row_ready, 1)
            squares(1, lambda tt: act.wait_ge(x_ready, 2 * tt + 2))
            roots(1)
            spread_norm(1, 4, mod_a[:, KD:2 * KD], mod_t[:, Q_SHIFT_F:])
            act.wait_ge(soft_in, 1)
            f(prob, logit, ACT.Exp).then_inc(exp_ready, 1)
            act.wait_ge(lam_sums, 2)
            f(lam_s[:, 2:4], lam_s[:, 0:2], ACT.Exp).then_inc(lam_exps, 1)
            for k in range(0, KD, 2):
                act.wait_ge(gathered, k + 1)
                f(xet[:, k, :], bank(4 + k % 4), ACT.Identity, scale=mod_a[:, KD + k:KD + k + 1],
                  bias=mod_t[:, Q_SHIFT_F + k:Q_SHIFT_F + k + 1]).then_inc(xet_act, 1)

            with act.Fori(0, NE // 2) as i:
                for h in range(2):
                    act.wait_ge(gw_turned, 2 * i + (h + 1))
                    f(gwt, bank(2, t=4, m=P)[:, 0:TT, :], ACT.Copy).then_inc(gwt_ready, 1)
                    act.wait_ge(slot_used, 2 * EXPERT_SLOTS * i + (HEAD_SLOTS + h * EXPERT_SLOTS + 8))
                    f(sig_a, bank(0), ACT.Sigmoid).then_inc(sig_ready, 1)
                    act.wait_ge(act_turned, 2 * i + (h + 1))
                    f(act_t, bank(0, c=4, m=P), ACT.Copy).then_inc(act_t_ready, 1)
                    act.wait_ge(slot_used, 2 * EXPERT_SLOTS * i + (HEAD_SLOTS + (h + 1) * EXPERT_SLOTS))
                    f(y[:, 0, :], bank(2), ACT.Copy).then_inc(y_act, 1)

            act.wait_ge(pt_turned, 1)
            f(pt, bank(3, c=2, s=SEQ), ACT.Copy).then_inc(pt_ready, 1)
            squares(2, lambda tt: act.wait_ge(x_ready, 4 + 2 * tt + 2))
            roots(2)
            for b in (0, 2):
                act.wait_ge(slot_used, first_slot["w_pp"] + 1)
                f(pp[:, b // 2, 0:BANK], bank(b), ACT.Copy).then_inc(tfree[b], 1)
            squares(3, lambda tt: act.wait_ge(x_ready, 8 + tt + 1))
            roots(3)
            spread_norm(2, 4, col[:, C_MIX2:C_MIX2 + KD], None)

            def exponentials(a):
                act.wait_ge(max_ready, a + 1)
                s = scores[a % 2]
                for hh in range(8):
                    ins = f(s[:, hh, :], s[:, hh, :], ACT.Exp, bias=soft[:, a, 0, hh:hh + 1], accum_out=soft[:, a, 1, hh:hh + 1])
                ins.then_inc(exps_done, 1)

            for u, (name, _) in enumerate(TAIL_UNITS):
                b = 2 * (u % 2)
                if name in ("q_diff", "k_diff", "q_dil", "k_dil"):
                    i = ("q_diff", "k_diff", "q_dil", "k_dil").index(name)
                    for tt in range(TT):
                        await_bank(act, "tail", u, tt)
                        if i:
                            act.wait_ge(qk_mean, i)
                        f(sqt[:, tt, :], bank(b + tt), ACT.Square).then_inc(qk_squared, 1)
                        f(qn[i][:, tt, :], bank(b + tt), ACT.Copy).then_inc(tfree[b + tt], 1)
                    act.wait_ge(qk_mean, i + 1)
                    f(head_stat[:, 2, :], head_stat[:, 1, :], ACT.Sqrt).then_inc(qk_root, 1)
                elif name.startswith("turn_q"):
                    i = int(name == "turn_q_dil")
                    act.wait_ge(memset_done, 7)
                    await_bank(act, "tail", u, 0)
                    for c in range(2):
                        r = slice(c * DH, (c + 1) * DH)
                        ins = f(qz[i][r, 0:2, c, :], bank(b, c=2, s=SEQ)[r], ACT.Copy, scale=gain[r, 2 * i:2 * i + 1])
                    ins.then_inc(tfree[b], 1)
                elif name.startswith("turn_k"):
                    i = int(name == "turn_k_dil")
                    await_bank(act, "tail", u, 0)
                    f(kt[i][:, 0:2, :], bank(b, c=2, s=SEQ), ACT.Copy, scale=gain[:, 2 * i + 1:2 * i + 2]).then_inc(tfree[b], 1)
                elif name in ("v_diff", "v_dil"):
                    at = 512 * (name == "v_dil")
                    await_bank(act, "tail", u, 0)
                    f(v[:, 0, at:at + 512], bank(b), ACT.Copy).then_inc(tfree[b], 1)
                elif name in ("z0", "z1"):
                    n = int(name[1])
                    if n:
                        await_read(act, tfree, tail_u["z0"])
                    for j in range(2):
                        await_bank(act, "tail", u, j)
                        f(sgz[:, 2 * j:2 * j + 2, :], bank(b + j, c=2, s=SEQ), ACT.Sigmoid).then_inc(sgz_ready, 1)
                elif name.startswith(("turn_w", "turn_e")):
                    i = {"turn_w0": 0, "turn_w1": 8, "turn_e0a": 0, "turn_e0b": 8, "turn_e1a": 0, "turn_e1b": 8}[name]
                    await_bank(act, "tail", u, 0)
                    f(wt[:, i:i + 4, :], bank(b, i=4, m=P), ACT.Copy).then_inc(tfree[b], 1)
                elif name == "pv_diff":
                    for tt in range(TT):
                        await_bank(act, "tail", u, tt)
                        f(sqt[:, tt, :], bank(b + tt), ACT.Square).then_inc(qk_squared, 1)
                        f(cat[:, tt, 0:512], bank(b + tt), ACT.Copy).then_inc(tfree[b + tt], 1)
                    act.wait_ge(qk_mean, 5)
                    f(head_stat[:, 2, 0:8], head_stat[:, 1, 0:8], ACT.Sqrt).then_inc(qk_root, 1)
                if name in SCORES_AFTER:
                    exponentials(SCORES_AFTER[name])

            def out_read(tt):
                await_read(act, tfree, OUT_UNIT + tt)
            squares(4, out_read)
            roots(4)
            spread_norm(3, 4, col[:, C_PLE:C_PLE + KD], None)
            act.wait_ge(slot_used, first_slot["w_gate"] + 4)
            for tt in range(TT):
                for n in range(2):
                    f(gt[:, tt, n * BANK:(n + 1) * BANK], bank(2 * ((GATE_UNIT + tt) % 2) + n), ACT.Sigmoid).then_inc(gate_sig, 1)

        @block.vector
        def _(dve):
            count = [0]
            V = nc.vector

            def link(ins):
                count[0] += 1
                ins.then_inc(dve_chain, 1)
                dve.wait_ge(dve_chain, count[0])

            def norm_rows(n, turned):
                dve.wait_ge(squared, 2 * n + 2)
                V.tensor_scalar(stat[:, n, 1, :], stat[:, n, 0, :], 1.0 / D, EPS, ALU.mult, ALU.add).then_inc(mean_ready, 1)
                dve.wait_ge(root_ready, n + 1)
                link(V.reciprocal(stat[:, n, 3, :], stat[:, n, 2, :]))
                if turned:
                    for tt in range(TT):
                        V.tensor_scalar(xr[:, tt, :], x[:, tt, :], stat[:, n, 3, tt:tt + 1], None, ALU.mult).then_inc(xr_ready, 1)

            def spread_norm(n, first_bank, scale, shift, sems=None):
                for q in (1, 3):
                    dve.wait_ge(norm_turned, 4 * n + q + 1)
                    for c in range(2):
                        k = 2 * q + c
                        src = bank(first_bank + q, c=2, s=SEQ)[:, c, :]
                        if shift is None:
                            ins = V.tensor_scalar(ht[:, k, :], src, scale[:, k:k + 1], None, ALU.mult)
                        else:
                            ins = V.tensor_scalar(ht[:, k, :], src, scale[:, k:k + 1], shift[:, k:k + 1], ALU.mult, ALU.add)
                    ins.then_inc(sems[q] if sems else norm_dve, 1)

            def modulation_columns(b, from_bank):
                dve.wait_ge(mod_turned, b + 1)
                src = bank(from_bank, c=4, g=4, r=32)[:, :, :, 0].rearrange("p c g -> p g c")
                at = slice(16 * b, 16 * b + 16)
                link(V.tensor_tensor(shaped(mod_t[:, at], g=4, c=4), src, shaped(col[:, C_BADA + 16 * b:C_BADA + 16 * b + 16], g=4, c=4), ALU.add))

            dve.wait_ge(x_loaded, 16)
            norm_rows(0, True)
            dve.wait_ge(vec_turned, 1)
            V.tensor_copy(col, psum[:, 7, 0:P]).then_inc(vec_ready, 1)
            dve.wait_ge(vec_ready, 1)
            dve.wait_ge(sig_c_ready, 1)
            link(V.tensor_tensor(c_act, col[:, C_C:C_C + KD], sig_c, ALU.mult))
            V.tensor_copy(c_rep, c_act.unsqueeze(2).broadcast_to([P, KD, 32])).then_inc(c_ready, 1)
            dve.wait_ge(lam_loaded, 64)
            for n in range(2):
                link(V.tensor_tensor(lam_in[:, 2 * n, :], lam_in[:, 2 * n, :], lam_in[:, 2 * n + 1, :], ALU.mult))
                V.tensor_reduce(lam_s[:, n:n + 1], lam_in[:, 2 * n, :], AX.X, ALU.add).then_inc(lam_sums, 1)
            modulation_columns(0, 5)
            V.scalar_tensor_tensor(mod_a[:, 0:KD], mod_t[:, Q_SCALE_M:Q_SCALE_M + KD], 1.0, col[:, C_GMIX:C_GMIX + KD],
                                   ALU.add, ALU.mult).then_inc(mod_ready, 1)
            dve.wait_ge(mod_ready, 1)
            spread_norm(0, 0, mod_a[:, 0:KD], mod_t[:, Q_SHIFT_M:], free)

            for u, (name, _) in enumerate(HEAD_UNITS):
                b = 2 * (u % 2)
                if name == "fourier_in":
                    await_bank(dve, "head", u, 1)
                    V.tensor_copy(u_rows[:, 1, :], bank(b + 1)).then_inc(free[b + 1], 1)
                elif name in ("v0", "v1"):
                    await_bank(dve, "head", u, 1)
                    V.tensor_copy(vt[:, 2:4, :], bank(b + 1, c=2, s=SEQ)).then_inc(free[b + 1], 1)
                elif name in ("seq01", "seq23"):
                    await_bank(dve, "head", u, 1)
                    V.tensor_copy(ab[:, 2 * (name == "seq23") + 1, :], bank(b + 1)).then_inc(free[b + 1], 1)
                elif name == "group":
                    await_bank(dve, "head", u, 1)
                    V.tensor_copy(fm[:, 2:4, :], bank(b + 1, c=2, s=SEQ)).then_inc(free[b + 1], 1)
                elif name in ("c0", "c1"):
                    await_read(dve, free, head_u["v" + name[1]])
                    dve.wait_ge(memset_done, 3)
                    for j in range(2):
                        await_bank(dve, "head", u, j)
                        V.tensor_tensor(cv[:, 2 * j:2 * j + 2, 1:SEQ + 1], bank(b + j, c=2, s=SEQ), vt[:, 2 * j:2 * j + 2, :],
                                        ALU.mult).then_inc(free[b + j], 1)
                    await_read(dve, free, u)
                    for tap in range(3):
                        for c in range(4):
                            w = C_CONV + tap * KD + 4 * int(name[1]) + c
                            src = cv[:, c, tap:tap + SEQ]
                            if tap == 0:
                                ins = V.tensor_scalar(conv[:, c, :], src, col[:, w:w + 1], None, ALU.mult)
                            else:
                                ins = V.scalar_tensor_tensor(conv[:, c, :], src, col[:, w:w + 1], conv[:, c, :], ALU.mult, ALU.add)
                        link(ins)
                elif name in ("b0", "b1"):
                    for j in range(2):
                        await_bank(dve, "head", u, j)
                        k = 4 * int(name[1]) + 2 * j
                        V.tensor_tensor(st[:, k:k + 2, :], bank(b + j, c=2, s=SEQ), conv[:, 2 * j:2 * j + 2, :], ALU.mult).then_inc(free[b + j], 1)
                elif name in ("ya0", "ya1"):
                    await_read(dve, free, head_u["ga" + name[2]])
                    for j in range(2):
                        await_bank(dve, "head", u, j)
                        k = 4 * int(name[2]) + 2 * j
                        V.tensor_tensor(ga[:, k:k + 2, :], bank(b + j, c=2, s=SEQ), ga[:, k:k + 2, :], ALU.mult).then_inc(free[b + j], 1)
                elif name in ("yb0", "yb1"):
                    await_read(dve, free, head_u["gb" + name[2]])
                    await_read(dve, free, head_u["ya" + name[2]])
                    for j in range(2):
                        await_bank(dve, "head", u, j)
                        k = 4 * int(name[2]) + 2 * j
                        link(V.tensor_tensor(gb[:, k:k + 2, :], bank(b + j, c=2, s=SEQ), gb[:, k:k + 2, :], ALU.mult))
                        V.tensor_tensor(ga[:, k:k + 2, :], ga[:, k:k + 2, :], gb[:, k:k + 2, :], ALU.add).then_inc(free[b + j], 1)
            dve.wait_ge(gain_turned, 1)
            V.tensor_copy(gain[:, 0:5], psum[:, 6, 0:5]).then_inc(gain_ready, 1)
            dve.wait_ge(gain_ready, 1)
            V.tensor_scalar(sub_gain, gain[:, 4:5], 1.0 - LAM_INIT, None, ALU.mult)
            modulation_columns(1, 6)
            modulation_columns(2, 7)

            def diagonal(g, q):
                for k in range(KD):
                    ins = V.tensor_scalar(diag[g][:, k * P:(k + 1) * P], ident, mod_t[:, q + k:q + k + 1], None, ALU.mult)
                ins.then_inc(diag_ready, 1)

            diagonal(0, Q_GATE_M)
            diagonal(1, Q_GATE_F)
            V.scalar_tensor_tensor(mod_a[:, KD:2 * KD], mod_t[:, Q_SCALE_F:Q_SCALE_F + KD], 1.0, col[:, C_GMOE:C_GMOE + KD],
                                   ALU.add, ALU.mult).then_inc(mod_ready, 1)
            dve.wait_ge(gate_row_ready, 2)
            dve.wait_ge(slot_used, first_slot["w_o"] + WO)
            for tt in range(TT):
                for n in range(2):
                    b = 2 * ((MIX_UNIT + tt) % 2) + n
                    cols = slice(n * BANK, (n + 1) * BANK)
                    if tt:
                        dve.wait_ge(x_ready, n + 1)
                    V.tensor_tensor(mix_tmp[:, n, :], bank(b), gm_row[:, cols], ALU.mult).then_inc(free[b], 1)
                    dve.wait_ge(free[b], (MIX_UNIT + tt) // 2 + 2)
                    V.tensor_tensor(x[:, tt, cols], x[:, tt, cols], mix_tmp[:, n, :], ALU.add).then_inc(x_ready, 1)
            dve.wait_ge(x_ready, 4)
            norm_rows(1, True)
            dve.wait_ge(mod_ready, 2)
            spread_norm(1, 4, mod_a[:, KD:2 * KD], mod_t[:, Q_SHIFT_F:])

            dve.wait_ge(logits_done, 1)
            dve.wait_ge(side_loaded, 64)
            link(V.tensor_tensor(logit, bank(0)[:, 0:32].rearrange("p (t e) -> p t e", t=TT), br.unsqueeze(1).broadcast_to([P, TT, NE]), ALU.add))
            link(V.tensor_reduce(route[:, 0, :], logit, AX.X, ALU.max))
            V.tensor_tensor(logit, logit, route[:, 0, :].unsqueeze(2).broadcast_to([P, TT, NE]), ALU.subtract).then_inc(soft_in, 1)
            dve.wait_ge(exp_ready, 1)
            link(V.tensor_reduce(route[:, 1, :], prob, AX.X, ALU.add))
            link(V.reciprocal(route[:, 2, :], route[:, 1, :]))
            V.tensor_tensor(prob, prob, route[:, 2, :].unsqueeze(2).broadcast_to([P, TT, NE]), ALU.mult).then_inc(prob_ready, 1)
            dve.wait_ge(prob_turned, 1)
            link(V.tensor_copy(left_t[0:NE, :], psum[0:NE, 1, 0:SEQ]))
            for _ in range(CAP // 8):
                link(V.max(top8[0:NE, :], left_t[0:NE, :]))
                link(V.match_replace(left_t[0:NE, :], top8[0:NE, :], left_t[0:NE, :], -1.0))
            V.tensor_scalar(left_t[0:NE, :], left_t[0:NE, :], 0.0, None, ALU.is_lt).then_inc(mask_ready, 1)
            dve.wait_ge(mask_turned, 1)
            V.tensor_copy(sel, bank(2)[:, 0:32].rearrange("p (t e) -> p t e", t=TT)).then_inc(sel_ready, 1)
            dve.wait_ge(sel_ready, 1)
            dve.wait_ge(slots_done, 1)
            link(V.scalar_tensor_tensor(slot_of, sel, -UNPICKED, bank(3)[:, 0:32].rearrange("p (t e) -> p t e", t=TT), ALU.mult, ALU.add))
            for tt in range(TT):
                V.tensor_tensor(pick[:, tt], slot_of[:, tt, :].unsqueeze(2).broadcast_to([P, NE, CAP]),
                                slot_no.unsqueeze(1).broadcast_to([P, NE, CAP]), ALU.is_equal).then_inc(pick_ready, 1)
            dve.wait_ge(prob_ready, 1)
            dve.wait_ge(pick_ready, 2)
            for tt in range(TT):
                V.tensor_tensor(weigh[:, tt], pick[:, tt], prob[:, tt, :].unsqueeze(2).broadcast_to([P, NE, CAP]), ALU.mult).then_inc(pick_ready, 1)
            V.memset(zero, 0.0).then_inc(pick_ready, 1)
            for k in range(1, KD, 2):
                dve.wait_ge(gathered, k + 1)
                V.tensor_scalar(xet[:, k, :], bank(4 + k % 4), mod_a[:, KD + k:KD + k + 1], mod_t[:, Q_SHIFT_F + k:Q_SHIFT_F + k + 1],
                                ALU.mult, ALU.add).then_inc(xet_dve, 1)

            with dve.Fori(0, NE // 2) as i:
                for h in range(2):
                    dve.wait_ge(sig_ready, 2 * i + (h + 1))
                    V.tensor_tensor(sig_a, bank(0), sig_a, ALU.mult).then_inc(gated, 1)
                    dve.wait_ge(gated, 2 * i + (h + 1))
                    dve.wait_ge(slot_used, 2 * EXPERT_SLOTS * i + (HEAD_SLOTS + h * EXPERT_SLOTS + 16))
                    V.tensor_tensor(act_h, bank(1), sig_a, ALU.mult).then_inc(act_ready, 1)
                    dve.wait_ge(slot_used, 2 * EXPERT_SLOTS * i + (HEAD_SLOTS + (h + 1) * EXPERT_SLOTS))
                    V.tensor_copy(y[:, 1, :], bank(3)).then_inc(y_dve, 1)

            dve.wait_ge(scattered, NE)
            dve.wait_ge(gate_row_ready, 4)
            for tt in range(TT):
                for n in range(2):
                    cols = slice(n * BANK, (n + 1) * BANK)
                    link(V.tensor_tensor(y[:, n, :], bank(4 + 2 * tt + n), gf_row[:, cols], ALU.mult))
                    V.tensor_tensor(x[:, tt, cols], x[:, tt, cols], y[:, n, :], ALU.add).then_inc(x_ready, 1)
            dve.wait_ge(x_ready, 8)
            norm_rows(2, False)
            for tt in range(TT):
                V.scalar_tensor_tensor(x[:, tt, :], x[:, tt, :], stat[:, 2, 3, tt:tt + 1], gfin, ALU.mult, ALU.mult).then_inc(x_ready, 1)
            for b in (1, 3):
                dve.wait_ge(slot_used, first_slot["w_pp"] + 1)
                V.tensor_copy(pp[:, b // 2, BANK:2 * BANK], bank(b)).then_inc(tfree[b], 1)
            dve.wait_ge(lam_exps, 1)
            link(V.tensor_tensor(lam_s[:, 4:5], lam_s[:, 3:4], lam_s[:, 2:3], ALU.subtract))
            link(V.tensor_scalar(lam_s[:, 5:6], lam_s[:, 4:5], LAM_INIT, None, ALU.subtract))
            dve.wait_ge(x_ready, 10)
            norm_rows(3, True)
            spread_norm(2, 4, col[:, C_MIX2:C_MIX2 + KD], None)

            def head_roots(n, width, heads, target):
                dve.wait_ge(qk_squared, 2 * n + 2)
                nh = TT * heads
                for tt in range(TT):
                    ins = V.tensor_reduce(head_stat[:, 0, tt * heads:(tt + 1) * heads], shaped(sqt[:, tt, :], h=heads, e=width), AX.X, ALU.add)
                link(ins)
                V.tensor_scalar(head_stat[:, 1, 0:nh], head_stat[:, 0, 0:nh], 1.0 / width, EPS, ALU.mult, ALU.add).then_inc(qk_mean, 1)
                dve.wait_ge(qk_root, n + 1)
                link(V.reciprocal(head_stat[:, 3, 0:nh], head_stat[:, 2, 0:nh]))
                for tt in range(TT):
                    rows = target(tt).rearrange("p (h e) -> p h e", h=heads)
                    r = head_stat[:, 3, tt * heads:(tt + 1) * heads].unsqueeze(2).broadcast_to([P, heads, width])
                    V.tensor_tensor(rows, rows, r, ALU.mult).then_inc(qn_ready if n < 4 else cat_ready, 1)

            def score_max(a):
                s = scores[a % 2]
                dve.wait_ge(bias_loaded, 16)
                for j in range(4):
                    dve.wait_ge(scores_done, 4 * a + j + 1)
                    if a < 2:
                        pos = bias[:, a % 2, j, :].unsqueeze(1).broadcast_to([P, 2, SEQ])
                    else:
                        pos = bias[:, a % 2, 4 + 2 * j:6 + 2 * j, :]
                    V.scalar_tensor_tensor(s[:, 2 * j:2 * j + 2, :], bank(4 + j, c=2, s=SEQ), SCALE, pos, ALU.mult, ALU.add).then_inc(scores_read, 1)
                dve.wait_ge(scores_read, 4 * a + 4)
                V.tensor_reduce(soft[:, a, 0, :], s, AX.X, ALU.max, negate=True).then_inc(max_ready, 1)

            def diff_weights(a):
                s = scores[a]
                dve.wait_ge(exps_done, a + 1)
                link(V.reciprocal(soft[:, a, 2, :], soft[:, a, 1, :]))
                link(V.tensor_scalar(soft[:, a, 3, :], soft[:, a, 2, :], lam_s[:, 5:6], None, ALU.mult))
                for hh in range(4):
                    ins = V.tensor_scalar(s[:, 2 * hh, :], s[:, 2 * hh, :], soft[:, a, 2, 2 * hh:2 * hh + 1], None, ALU.mult)
                link(ins)
                for hh in range(4):
                    ins = V.scalar_tensor_tensor(s[:, 2 * hh, :], s[:, 2 * hh + 1, :], soft[:, a, 3, 2 * hh + 1:2 * hh + 2], s[:, 2 * hh, :],
                                                 ALU.mult, ALU.add)
                ins.then_inc(w_ready, 1)

            for u, (name, _) in enumerate(TAIL_UNITS):
                b = 2 * (u % 2)
                if name in ("q_diff", "k_diff", "q_dil", "k_dil"):
                    i = ("q_diff", "k_diff", "q_dil", "k_dil").index(name)
                    await_read(dve, tfree, u)
                    head_roots(i, DH, 8, lambda tt: qn[i][:, tt, :])
                elif name.startswith("turn_q"):
                    i = int(name == "turn_q_dil")
                    dve.wait_ge(memset_done, 7)
                    await_bank(dve, "tail", u, 1)
                    for c in range(2):
                        r = slice(c * DH, (c + 1) * DH)
                        ins = V.tensor_scalar(qz[i][r, 2:4, c, :], bank(b + 1, c=2, s=SEQ)[r], gain[r, 2 * i:2 * i + 1], None, ALU.mult)
                    ins.then_inc(tfree[b + 1], 1)
                elif name.startswith("turn_k"):
                    i = int(name == "turn_k_dil")
                    await_bank(dve, "tail", u, 1)
                    V.tensor_scalar(kt[i][:, 2:4, :], bank(b + 1, c=2, s=SEQ), gain[:, 2 * i + 1:2 * i + 2], None, ALU.mult).then_inc(tfree[b + 1], 1)
                elif name in ("v_diff", "v_dil"):
                    at = 512 * (name == "v_dil")
                    await_bank(dve, "tail", u, 1)
                    V.tensor_copy(v[:, 1, at:at + 512], bank(b + 1)).then_inc(tfree[b + 1], 1)
                elif name in ("z0", "z1"):
                    n = int(name[1])
                    for j in range(2):
                        dve.wait_ge(sgz_ready, 2 * n + j + 1)
                        k = 4 * n + 2 * j
                        V.tensor_tensor(szt[:, k:k + 2, :], bank(b + j, c=2, s=SEQ), sgz[:, 2 * j:2 * j + 2, :], ALU.mult).then_inc(tfree[b + j], 1)
                elif name.startswith(("turn_w", "turn_e")):
                    i = {"turn_w0": 4, "turn_w1": 12, "turn_e0a": 4, "turn_e0b": 12, "turn_e1a": 4, "turn_e1b": 12}[name]
                    await_bank(dve, "tail", u, 1)
                    V.tensor_copy(wt[:, i:i + 4, :], bank(b + 1, i=4, m=P)).then_inc(tfree[b + 1], 1)
                elif name == "pv_diff":
                    await_read(dve, tfree, u)
                    head_roots(4, P, 4, lambda tt: cat[:, tt, 0:512])
                elif name.startswith("pv_dil"):
                    tt = int(name[6])
                    dve.wait_ge(exps_done, 3 + tt)
                    link(V.reciprocal(soft[:, 2 + tt, 2, :], soft[:, 2 + tt, 1, :]))
                    for j in range(2):
                        await_bank(dve, "tail", u, j)
                        r = soft[:, 2 + tt, 2, 4 * j:4 * j + 4].unsqueeze(2).broadcast_to([P, 4, DH])
                        V.tensor_tensor(cat[:, tt, 512 + 256 * j:768 + 256 * j].rearrange("p (h e) -> p h e", h=4),
                                        bank(b + j)[:, 0:256].rearrange("p (h e) -> p h e", h=4), r, ALU.mult).then_inc(tfree[b + j], 1)
                elif name.startswith("turn_cat"):
                    i = int(name[-1])
                    await_read(dve, tfree, tail_u[f"z{i}"])
                    for j in range(2):
                        await_bank(dve, "tail", u, j)
                        k = 4 * i + 2 * j
                        if i == 0:
                            ins = V.scalar_tensor_tensor(ht[:, k:k + 2, :], bank(b + j, c=2, s=SEQ), sub_gain, szt[:, k:k + 2, :], ALU.mult, ALU.mult)
                        else:
                            ins = V.tensor_tensor(ht[:, k:k + 2, :], bank(b + j, c=2, s=SEQ), szt[:, k:k + 2, :], ALU.mult)
                        ins.then_inc(tfree[b + j], 1)
                if name in SCORES_AFTER:
                    score_max(SCORES_AFTER[name])
                if name in ("k_dil", "v_dil"):
                    diff_weights(("k_dil", "v_dil").index(name))
            dve.wait_ge(slot_used, first_slot["w_out"] + 4)
            for tt in range(TT):
                for n in range(2):
                    b = 2 * ((OUT_UNIT + tt) % 2) + n
                    cols = slice(n * BANK, (n + 1) * BANK)
                    V.tensor_tensor(x[:, tt, cols], x[:, tt, cols], bank(b), ALU.add).then_inc(tfree[b], 1)
            await_read(dve, tfree, OUT_UNIT)
            await_read(dve, tfree, OUT_UNIT + 1)
            norm_rows(4, True)
            spread_norm(3, 4, col[:, C_PLE:C_PLE + KD], None)
            for tt in range(TT):
                for n in range(2):
                    cols = slice(n * BANK, (n + 1) * BANK)
                    dve.wait_ge(gate_sig, 2 * tt + n + 1)
                    link(V.tensor_tensor(gt[:, tt, cols], gt[:, tt, cols], pp[:, tt, cols], ALU.mult))
                    V.tensor_tensor(x[:, tt, cols], x[:, tt, cols], gt[:, tt, cols], ALU.add).then_inc(out_ready, 1)


def vec_sources(t):
    found = [(C_C, t["c"].rearrange("b (k p) -> (b k) p", p=P))]
    for at, name in ((C_GMIX, "g_norm_mix"), (C_GMOE, "g_norm_moe"), (C_MIX2, "mix_norm_g_2"), (C_PLE, "ple_norm_g_2"),
                     (C_BADA, "b_ada"), (C_BGATE, "b_gate")):
        found.append((at, t[name].rearrange("b (k p) -> (b k) p", p=P)))
    found.append((C_CONV, t["w_conv"][0].rearrange("w (k p) -> (w k) p", p=P)))
    return found


VEC_DMAS = 8

_INS = ["x", "c", "w_ada", "b_ada", "g_norm_mix", "w_in", "b_gate", "w_fourier", "w_conv", "w_conv_out", "w_o",
        "g_norm_moe", "w_router", "b_router", "w_gate_e", "w_up_e", "w_down_e", "g_final", "p_2", "mix_norm_g_2",
        "w_in_2", "diff_q_norm_g_2", "diff_k_norm_g_2", "lambda_q1_2", "lambda_k1_2", "lambda_q2_2", "lambda_k2_2",
        "diff_sub_norm_g_2", "dil_q_norm_g_2", "dil_k_norm_g_2", "w_out_2", "ple_norm_g_2", "w_ple_gate_2",
        "w_ple_proj_2"]


def kernel(**inputs):
    import concourse.bacc as bacc
    from concourse.bass_utils import run_bass_kernel_spmd

    nc = bacc.Bacc("TRN2", target_bir_lowering=False, num_devices=1)
    arrays, tensors = {}, {}
    for name, a in list({n: inputs[n] for n in _INS}.items()) + list(shape_constants().items()):
        a = np.ascontiguousarray(a)
        arrays[f"in_{name}"] = a
        tensors[name] = nc.dram_tensor(f"in_{name}", a.shape, mybir.dt.from_np(a.dtype), kind="ExternalInput").ap()
    out = nc.dram_tensor("out", (1, SEQ, D), F32, kind="ExternalOutput").ap()
    build(nc, tensors, out)
    return run_bass_kernel_spmd(nc, [arrays], core_ids=[0]).results[0]["out"]
```

```python
from contextlib import ExitStack

import numpy as np

import concourse.bass as bass
from concourse import mybir

F32 = mybir.dt.float32
F32R = mybir.dt.float32r
ALU = mybir.AluOpType
ACT = mybir.ActivationFunctionType
AX = mybir.AxisListType

P = 128
SEQ, D = 256, 1024
TT = SEQ // P
KD = D // P
BANK = 512
DF = 512
FG = DF // P
NE, CAP, DE = 16, 32, 2048
SLOT = 2048
RING = 16
EPS = 1e-6
UNPICKED = 1000.0
LAM_INIT = 0.2
DH = 64
SCALE = DH ** -0.5

ADA0, WIN, ADA1, ADA2, WF, WCO, WO = 8, 22, 8, 8, 2, 4, 4
HALF = BANK // 2
HEAD_SLOTS = ADA0 + WIN + ADA1 + ADA2 + WF + WCO + WO
EXPERT_SLOTS = 24
HEAD_PARTS, HEAD_RING = 4, RING - 4
TAIL_ROOM, TAIL_PARTS = 8, 3
TAIL_RING = RING - TAIL_ROOM - TAIL_PARTS
FIRST_TAIL = HEAD_SLOTS + NE * EXPERT_SLOTS

C_C, C_GMIX, C_GMOE, C_MIX2, C_PLE, C_BADA, C_BGATE, C_CONV = 0, 8, 16, 24, 32, 40, 88, 104
Q_SHIFT_M, Q_SCALE_M, Q_GATE_M, Q_SHIFT_F, Q_SCALE_F, Q_GATE_F = 0, 8, 16, 24, 32, 40


def shape_constants():
    s = np.arange(SEQ)
    a = 2 * np.pi * np.outer(s, s) / SEQ
    dft_seq = np.concatenate([np.cos(a), np.sin(a)], 1) / np.sqrt(SEQ)
    g = np.arange(P)
    b = 2 * np.pi * np.outer(g, g) / P
    dft_group = np.concatenate([np.cos(b), -np.sin(b)], 1) / np.sqrt(P)
    before = (g[:, None] < g[None, :]).astype(np.float32)
    slots = np.broadcast_to(np.arange(CAP) - UNPICKED, (P, CAP))
    small = np.concatenate([np.eye(P), before, slots], 1)
    dist = np.abs(s[:, None] - s[None, :])
    count = np.zeros((SEQ, SEQ))
    for window, dilation in ((128, 1), (512, 4), (2048, 16)):
        count += (dist % dilation == 0) & (dist // dilation <= window // (2 * dilation))
    log_count = np.where(count > 0, np.log(np.maximum(count, 1)), -1e30)
    diff = [-(2.0 ** (-8.0 * (h + 1) / 4)) * dist for h in range(4)]
    dil = [-(2.0 ** (-8.0 * (h + 1) / 8)) * dist + log_count for h in range(8)]
    bias = np.stack(diff + dil, 1)
    return {n: np.ascontiguousarray(v, dtype=np.float32) for n, v in
            dict(dft_seq=dft_seq, dft_group=dft_group, small=small, bias=bias).items()}


HEAD_UNITS = [("fourier_in", 2), ("v0", 2), ("seq01", 0), ("c0", 2), ("seq23", 0), ("v1", 2),
              ("group", 0), ("b0", 2), ("c1", 2), ("b1", 2), ("ga0", 2), ("ga1", 2), ("ya0", 1), ("ya1", 1),
              ("gb0", 2), ("gb1", 2), ("yb0", 2), ("yb1", 2)]
MIX_UNIT = len(HEAD_UNITS)
TAIL_UNITS = [("q_diff", 2), ("k_diff", 2), ("turn_q_diff", 0), ("q_dil", 2), ("turn_k_diff", 0), ("k_dil", 2),
              ("turn_q_dil", 0), ("v_diff", 2), ("turn_k_dil", 0), ("v_dil", 2), ("turn_w0", 0), ("z0", 2),
              ("turn_w1", 0), ("pv_diff", 0), ("z1", 2), ("turn_e0a", 0), ("turn_e0b", 0), ("pv_dil0", 0),
              ("turn_cat0", 0), ("turn_e1a", 0), ("turn_e1b", 0), ("pv_dil1", 0), ("turn_cat1", 0)]
SCORES_AFTER = {"k_dil": 0, "turn_k_dil": 1, "turn_w0": 2, "pv_diff": 3}
ROWS_UNITS = ("fourier_in", "q_diff", "k_diff", "v_diff", "q_dil", "k_dil", "v_dil")
ADA_BEFORE = {u: [divmod(n, KD)] for n, u in enumerate(list(range(1, 13)))}
ADA_BEFORE |= {14: [divmod(12, KD), divmod(13, KD)], 15: [divmod(14, KD)], 16: [divmod(15, KD)]}
ADA_BEFORE = {u: [(1 + b, k) for b, k in steps] for u, steps in ADA_BEFORE.items()}
EXPS_AFTER = {"k_dil": 0, "turn_k_dil": 1, "turn_w1": 2, "turn_e0b": 3}
OUT_AFTER = "turn_e1b"
X_AFTER = 3
IN_CHUNK = {"fourier_in": 0, "v0": 1, "v1": 2, "b0": 3, "b1": 4, "c0": 5, "c1": 6, "ga0": 7, "ga1": 8, "gb0": 9, "gb1": 10}
IN2_CHUNK = {"q_diff": 0, "k_diff": 1, "v_diff": 2, "q_dil": 3, "k_dil": 4, "v_dil": 5, "z0": 6, "z1": 7}


def build(nc, t, out):
    ctx = ExitStack()
    with ctx:
        def sem(name):
            return ctx.enter_context(nc.semaphore(name))

        BASE = 16512
        ring = nc.alloc_sbuf_tensor_at("ring", [P, RING, SLOT], F32, offset=BASE)
        ring_r = [nc.alloc_sbuf_tensor_at(f"ring_r{p}", [P, SLOT], F32R, offset=BASE + p * SLOT * 4) for p in range(RING)]
        psum = ctx.enter_context(nc.psum_tensor("psum", [P, 8, BANK], F32))
        SIZE = 20400
        arena = nc.alloc_sbuf_tensor_at("arena", [P, SIZE], F32, offset=BASE + RING * SLOT * 4)
        top = [0]

        def own(n):
            at = top[0]
            top[0] += -(-n // 8) * 8
            return arena[:, at:at + n]

        def shaped(ap, **dims):
            names = list(dims)
            return ap.rearrange(f"p ({' '.join(names)}) -> p {' '.join(names)}", **dims)

        x = shaped(own(TT * D), t=TT, d=D)
        xr_at = top[0]
        xr_flat = own(TT * D)
        xr = shaped(xr_flat, t=TT, d=D)
        ht_at = top[0]
        ht_flat = own(TT * D)
        ht = shaped(ht_flat, k=KD, s=SEQ)
        small = own(P + P + CAP)
        ident, before, slot_no = small[:, 0:P], small[:, P:2 * P], small[:, 2 * P:2 * P + CAP]
        ones = own(P)
        col = own(P)
        gain = own(8)
        sub_gain = own(1)
        spare_root = own(1)
        c_act = own(KD)
        mod_t = own(48)
        mod_a = own(2 * KD)
        stat = shaped(own(5 * 4 * TT), n=5, c=4, t=TT)
        half_sum = shaped(own(8), i=2, n=2, t=TT)
        lam_in = shaped(own(4 * DH), v=4, d=DH)
        lam_s = own(8)
        soft = shaped(own(4 * 4 * 8), a=4, c=4, h=8)
        head_stat = shaped(own(4 * 16), c=4, h=16)
        cat_at = top[0]
        cat_flat = own(2 * D)
        gm_row, gf_row = cat_flat[:, 0:D], cat_flat[:, D:2 * D]
        cat = shaped(cat_flat, t=TT, d=D)
        gfin = own(D)
        stage = top[0]

        def area(at, n):
            assert stage + at + n <= SIZE, stage + at + n - SIZE
            return arena[:, stage + at:stage + at + n]

        def arena_at(at):
            return BASE + (RING * SLOT + at) * 4

        def parts(name, at, k):
            a = nc.alloc_sbuf_tensor_at(name, [P, k * SEQ], F32R, offset=arena_at(at))
            return shaped(a[:], k=k, s=SEQ)

        ht_hi, ht_lo = parts("ht_hi", ht_at, KD), parts("ht_lo", stage + 7688, KD)

        c_rep = shaped(area(0, 256), k=KD, r=32)
        dftg = area(256, 256)
        vt = shaped(area(512, 1024), k=4, s=SEQ)
        cv = shaped(area(1536, 4 * 258), k=4, s=258)
        conv = shaped(area(2568, 1024), k=4, s=SEQ)
        st_hi, st_lo = parts("st_hi", stage + 3592, KD), parts("st_lo", xr_at, KD)
        norm_tmp = shaped(area(3592, 2048), k=KD, s=SEQ)
        ga = shaped(area(5640, 2048), k=KD, s=SEQ)
        gb = [vt, conv]
        vec1, vec2, sig_c = area(3592, P), area(9736, P), area(3848, KD)
        mod_rows = [area(5640, BANK), area(1536, BANK), area(2048, BANK)]
        dfts = shaped(gfin, t=TT, n=2 * SEQ)
        u_rows = shaped(gm_row, t=TT, d=DF)
        ab = shaped(xr_flat, g=FG, s=2 * SEQ)
        fm_lo, fm_hi = parts("fm_lo", cat_at, FG), parts("fm_hi", cat_at + D, FG)
        mix_tmp = shaped(area(1536, 2 * BANK), j=2, c=BANK)
        diag_r = shaped(area(7168, 2 * P), t=TT, m=P)
        xet = shaped(area(0, KD * NE * CAP), k=KD, n=NE * CAP)
        cur = [shaped(area(4096 + 256 * h, 256), k=KD, s=CAP) for h in range(2)]
        gw_cur = [shaped(area(4608 + 256 * h, 256), t=TT, r=4, s=CAP) for h in range(2)]
        gwt = shaped(area(5120, 256), t=TT, m=P)
        sig_a = area(5376, BANK)
        act_h = area(5888, BANK)
        act_t = shaped(area(6400, BANK), c=4, m=P)
        y = shaped(area(6912, 2 * BANK), n=2, c=BANK)
        wr = shaped(area(9736, P), k=KD, e=NE)
        br = area(8064, NE)
        logit = shaped(area(8080, 32), t=TT, e=NE)
        prob = shaped(area(8112, 32), t=TT, e=NE)
        sel = shaped(area(8144, 32), t=TT, e=NE)
        slot_of = shaped(area(8176, 32), t=TT, e=NE)
        route = shaped(area(8208, 8), c=4, t=TT)
        prob_t = area(8216, SEQ)
        left_t = area(8472, SEQ)
        top8 = area(8728, 8)
        p_rows = shaped(area(8736, 512), t=TT, c=SEQ)
        rows_hi = shaped(nc.alloc_sbuf_tensor_at("rows_hi", [P, TT * D], F32R, offset=arena_at(xr_at))[:], t=TT, d=D)
        rows_lo = shaped(nc.alloc_sbuf_tensor_at("rows_lo", [P, TT * D], F32R, offset=arena_at(stage + 5120))[:], t=TT, d=D)
        rows_tmp = shaped(area(5120, TT * D), t=TT, d=D)
        pick_r = nc.alloc_sbuf_tensor_at("pick_r", [P, TT * NE * CAP], F32R, offset=arena_at(ht_at))[:]
        zero = nc.alloc_sbuf_tensor_at("zero", [P, BANK], mybir.dt.bfloat16, offset=arena_at(stage + 7424))[:]
        pick = shaped(pick_r, t=TT, e=NE, s=CAP)
        weigh = shaped(ht_flat[:, 1024:2048], t=TT, e=NE, s=CAP)
        weigh_flat = shaped(ht_flat[:, 1024:2048], t=TT, n=NE * CAP)
        pick_flat = shaped(pick_r, t=TT, n=NE * CAP)
        spare = ring[:, 0:TAIL_ROOM, :].rearrange("p a b -> p (a b)")
        bias = shaped(spare[:, 0:6144], t=TT, h=12, s=SEQ)
        qz = [shaped(spare[:, 6144 + 2048 * i:8192 + 2048 * i], k=4, c=2, s=SEQ) for i in range(2)]
        kt = [shaped(spare[:, 10240 + 1024 * i:11264 + 1024 * i], k=4, s=SEQ) for i in range(2)]
        v = shaped(spare[:, 12288:14336], t=TT, d=D)
        szt = shaped(spare[:, 14336:16384], k=KD, s=SEQ)
        s0_flat, wt_flat = area(0, 2048), area(2048, 2048)
        xg = shaped(s0_flat, t=TT, d=D)
        scores = [shaped(f, h=8, s=SEQ) for f in (xr_flat, s0_flat)]
        qn = [shaped(f, t=TT, c=512) for f in
              (wt_flat[:, 0:1024], wt_flat[:, 1024:2048], s0_flat[:, 0:1024], s0_flat[:, 1024:2048])]
        wt = shaped(wt_flat, i=16, m=P)
        pp = shaped(area(4096, 2048), t=TT, d=D)
        sqt = shaped(area(6144, 1024), t=TT, c=512)
        sgz = shaped(gfin, k=4, s=SEQ)
        pt = shaped(area(8192, 512), c=2, s=SEQ)
        gt = shaped(s0_flat, t=TT, d=D)

        def bank(b, **dims):
            return shaped(psum[:, b, :], **dims) if dims else psum[:, b, :]

        x_loaded, tables_loaded, vec_loaded, lam_loaded = (sem(n) for n in ("x_loaded", "tables_loaded", "vec_loaded", "lam_loaded"))
        gain_loaded, gain_turned, gain_ready = sem("gain_loaded"), sem("gain_turned"), sem("gain_ready")
        dft_loaded, side_loaded, bias_loaded = (sem(n) for n in ("dft_loaded", "side_loaded", "bias_loaded"))
        router_loaded, gate_bias_loaded = sem("router_loaded"), sem("gate_bias_loaded")
        loaded = [sem(f"slot{p}_loaded") for p in range(RING)]
        slot_used = sem("slot_used")
        memset_done = sem("memset_done")
        hi_ready, lo_ready, lo_pool_ready = sem("hi_ready"), sem("lo_ready"), sem("lo_pool_ready")
        vec_turned, vec_ready = sem("vec_turned"), sem("vec_ready")
        sig_c_ready, c_ready = sem("sig_c_ready"), sem("c_ready")
        mod_rows_ready, mod_turned, mod_ready = sem("mod_rows_ready"), sem("mod_turned"), sem("mod_ready")
        gate_row_done, gate_row_ready = sem("gate_row_done"), sem("gate_row_ready")
        squared, mean_ready, root_ready, scale_ready, xr_ready = (sem(n) for n in ("squared", "mean_ready", "root_ready", "scale_ready", "xr_ready"))
        norm_turned, norm_act, norm_dve = sem("norm_turned"), sem("norm_act"), sem("norm_dve")
        norm_spread, norm_hi, norm_lo = sem("norm_spread"), sem("norm_hi"), sem("norm_lo")
        fm_hi_ready, st_hi_ready, st_ready, z_hi_ready, z_ready = (sem(n) for n in ("fm_hi_ready", "st_hi_ready", "st_ready", "z_hi_ready", "z_ready"))
        x_ready, rows_ready = sem("x_ready"), sem("rows_ready")
        rows_hi_ready, zero_ready = sem("rows_hi_ready"), sem("zero_ready")
        first_ready, second_ready = sem("first_ready"), sem("second_ready")
        free = [sem(f"head_bank{b}_read") for b in range(4)]
        tfree = [sem(f"tail_bank{b}_read") for b in range(4)]
        dve_chain, act_chain, pool_chain = sem("dve_chain"), sem("act_chain"), sem("pool_chain")
        logits_done, exp_ready, prob_ready, prob_turned = (sem(n) for n in ("logits_done", "exp_ready", "prob_ready", "prob_turned"))
        soft_in = sem("soft_in")
        mask_ready, mask_turned, sel_ready, slots_done, pick_ready = (sem(n) for n in ("mask_ready", "mask_turned", "sel_ready", "slots_done", "pick_ready"))
        gathered, xet_act, xet_dve = sem("gathered"), sem("xet_act"), sem("xet_dve")
        cur_ready, gw_turned, gwt_ready = sem("cur_ready"), sem("gw_turned"), sem("gwt_ready")
        sig_ready, gated, act_ready, act_turned, act_t_ready = (sem(n) for n in ("sig_ready", "gated", "act_ready", "act_turned", "act_t_ready"))
        y_ready, scattered = sem("y_ready"), sem("scattered")
        pt_turned, pt_ready = sem("pt_turned"), sem("pt_ready")
        lam_sums, lam_exps = sem("lam_sums"), sem("lam_exps")
        qk_squared, qk_mean, qk_root, qn_ready = (sem(n) for n in ("qk_squared", "qk_mean", "qk_root", "qn_ready"))
        scores_done, scores_read, max_ready, exps_done, w_ready = (sem(n) for n in ("scores_done", "scores_read", "max_ready", "exps_done", "w_ready"))
        sgz_ready, cat_ready, yt_ready = sem("sgz_ready"), sem("cat_ready"), sem("yt_ready")
        yt_hi_ready = sem("yt_hi_ready")
        gate_sig, out_ready, stored = sem("gate_sig"), sem("out_ready"), sem("stored")

        def rows_of(w, cols, k0, nk):
            return w[k0 * P:(k0 + nk) * P, cols[0]:cols[1]].rearrange("(k p) n -> p k n", p=P)

        def columns(w, n, first=0):
            return [rows_of(w, ((first + i) * HALF, (first + i + 1) * HALF), 0, KD) for i in range(n)]

        w_ada, w_in, w_in2 = t["w_ada"][0], t["w_in"][0], t["w_in_2"][0]
        ada = [[rows_of(w_ada, (b * SLOT, (b + 1) * SLOT), k, 1) for k in range(KD)] for b in range(3)]
        head_stream = list(ada[0])
        first_slot = {f"ada0_{k}": k for k in range(KD)}
        for u, (name, _) in enumerate(HEAD_UNITS):
            for b, k in ADA_BEFORE.get(u, ()):
                first_slot[f"ada{b}_{k}"] = len(head_stream)
                head_stream.append(ada[b][k])
            first_slot[name] = len(head_stream)
            if name in IN_CHUNK:
                head_stream += columns(w_in, 2, 2 * IN_CHUNK[name])
            elif name in ("ya0", "ya1"):
                n = int(name[2])
                head_stream.append(rows_of(t["w_fourier"][0], (n * BANK, (n + 1) * BANK), 0, FG))
            elif name in ("yb0", "yb1"):
                head_stream += columns(t["w_conv_out"][0], 2, 2 * int(name[2]))
        first_slot["w_o"] = len(head_stream)
        head_stream += columns(t["w_o"][0], WO)
        assert len(head_stream) == HEAD_SLOTS
        tail_stream = [rows_of(t["w_ple_proj_2"][0], (0, D), 0, 2)]
        first_slot["w_pp"] = FIRST_TAIL
        for name, _ in TAIL_UNITS:
            if name in IN2_CHUNK:
                first_slot[name] = FIRST_TAIL + len(tail_stream)
                tail_stream += columns(w_in2, 2, 2 * IN2_CHUNK[name])
        first_slot["w_out"] = FIRST_TAIL + len(tail_stream)
        tail_stream += [rows_of(t["w_out_2"][0], (0, D), 2 * i, 2) for i in range(4)]
        first_slot["w_gate"] = FIRST_TAIL + len(tail_stream)
        tail_stream += columns(t["w_ple_gate_2"][0], 4)

        def place(s):
            if s < HEAD_SLOTS:
                return head_position(s), s // HEAD_RING + 1
            e = s - HEAD_SLOTS
            if s < FIRST_TAIL:
                return e % RING, head_loads(e % RING) + e // RING + 1
            n = s - FIRST_TAIL
            p = RING - TAIL_RING + n % TAIL_RING
            return p, head_loads(p) + NE * EXPERT_SLOTS // RING + n // TAIL_RING + 1

        def head_position(s):
            return (s - HEAD_SLOTS) % HEAD_RING

        def head_loads(p):
            return len([s for s in range(HEAD_SLOTS) if head_position(s) == p])

        def slot_in(s, **dims):
            return shaped(ring[:, place(s)[0], :], **dims)

        def arrived(eng, s):
            p, n = place(s)
            eng.wait_ge(loaded[p], 16 * n)

        head_split = [s for name, n in HEAD_UNITS if n for s in range(first_slot[name], first_slot[name] + n)]
        head_split += range(first_slot["w_o"], HEAD_SLOTS)
        tail_split = list(range(FIRST_TAIL + 1, FIRST_TAIL + len(tail_stream)))
        split_no = {s: n for n, s in enumerate(head_split + tail_split)}
        part_place = {s: HEAD_RING + n % HEAD_PARTS for n, s in enumerate(head_split)}
        part_place |= {s: TAIL_ROOM + n % TAIL_PARTS for n, s in enumerate(tail_split)}
        part_before = {s: head_split[n - HEAD_PARTS] for n, s in enumerate(head_split) if n >= HEAD_PARTS}
        part_before |= {s: tail_split[n - TAIL_PARTS] if n >= TAIL_PARTS else FIRST_TAIL - 1 for n, s in enumerate(tail_split)}

        def split_slots(units, after):
            seen, plan = 0, {}
            todo = [list(range(first_slot[name], first_slot[name] + n)) if n else [] for name, n in units] + [after]
            for u in range(len(units)):
                upto = next(n for n in range(u + 1, len(todo)) if todo[n])
                plan[u] = [s for n in range(max(seen, u) + 1, upto + 1) for s in todo[n]] if upto > seen else []
                seen = max(seen, upto)
            return plan

        ready_at = {}
        counts = {"first": 0, "second": 0}

        def plan(units, tag):
            for u, (name, slots) in enumerate(units):
                if slots == 2 and name not in ROWS_UNITS:
                    ready_at[tag, u, 0] = (slot_used, first_slot[name] + 1)
                else:
                    counts["first"] += 1
                    ready_at[tag, u, 0] = (first_ready, counts["first"])
                if slots:
                    ready_at[tag, u, 1] = (slot_used, first_slot[name] + slots)
                else:
                    counts["second"] += 1
                    ready_at[tag, u, 1] = (second_ready, counts["second"])

        plan(HEAD_UNITS, "head")
        plan(TAIL_UNITS, "tail")

        def await_bank(eng, tag, u, j):
            s, n = ready_at[tag, u, j]
            eng.wait_ge(s, n)

        def await_read(eng, sems, u):
            for j in range(2):
                eng.wait_ge(sems[2 * (u % 2) + j], u // 2 + 2)

        def gate_bank(c, tt):
            return (4 + c if c < 2 else c - 2) + 2 * tt

        head_u = {name: u for u, (name, _) in enumerate(HEAD_UNITS)}
        tail_u = {name: u for u, (name, _) in enumerate(TAIL_UNITS)}
        head_ahead = split_slots(HEAD_UNITS, [first_slot["w_o"], first_slot["w_o"] + 1])
        tail_ahead = split_slots(TAIL_UNITS[:tail_u["z1"] + 1], [first_slot["w_out"]])
        tail_ahead.pop(tail_u["z1"])
        ahead_late = {"turn_w1": tail_ahead.pop(tail_u["z0"]), "pv_dil0": [first_slot["w_out"]], "turn_cat0": [first_slot["w_out"] + 1],
                      "turn_e1b": [first_slot["w_out"] + 2]}
        pool_split = [s for s in tail_split if (s - FIRST_TAIL) % 2 == 0]
        block = ctx.enter_context(nc.Block())

        @block.sync
        def _(sp):
            for s, src in enumerate(head_stream):
                if s == X_AFTER:
                    sp.dma_start(x, t["x"][0].rearrange("(t p) d -> p t d", p=P)).then_inc(x_loaded, 16)
                if s == first_slot["v0"]:
                    sp.dma_start(dfts, t["dft_seq"].rearrange("(t p) n -> p t n", p=P)).then_inc(dft_loaded, 16)
                    sp.dma_start(dftg, t["dft_group"]).then_inc(dft_loaded, 16)
                if s == 2:
                    sp.wait_ge(vec_loaded, 16 * VEC_DMAS)
                if s >= HEAD_RING:
                    sp.wait_ge(slot_used, s - HEAD_RING + 1)
                sp.dma_start(slot_in(s, k=src.shape[1], n=src.shape[2]), src).then_inc(loaded[place(s)[0]], 16)
            with sp.Fori(0, NE // 2) as i:
                for h in range(2):
                    for j in range(EXPERT_SLOTS):
                        s = HEAD_SLOTS + h * EXPERT_SLOTS + j
                        w = t[("w_gate_e", "w_up_e", "w_down_e")[j // 8]][0]
                        w = w[bass.ds(2 * i + h, 1)]
                        if j < 16:
                            src = w[:, (j % 8) * P:(j % 8 + 1) * P, :].rearrange("e (k p) n -> p (e k) n", p=P)
                        else:
                            src = w[:, (j - 16) * 2 * P:(j - 15) * 2 * P, :].rearrange("e (k p) n -> p (e k) n", p=P)
                        before = HEAD_RING if s < HEAD_SLOTS + HEAD_RING else RING
                        sp.wait_ge(slot_used, 2 * EXPERT_SLOTS * i + (s - before + 1))
                        sp.dma_start(slot_in(s, k=src.shape[1], n=src.shape[2]), src).then_inc(loaded[place(s)[0]], 16)
            for n, src in enumerate(tail_stream):
                s = FIRST_TAIL + n
                sp.wait_ge(slot_used, FIRST_TAIL - TAIL_RING + n + 1 if n < TAIL_RING else s - TAIL_RING + 1)
                sp.dma_start(slot_in(s, k=src.shape[1], n=src.shape[2]), src).then_inc(loaded[place(s)[0]], 16)
            for c in range(4):
                sp.wait_ge(out_ready, TT * (c + 1))
                cols = slice(c * HALF, (c + 1) * HALF)
                sp.dma_start(out[0, :, cols].rearrange("(t p) d -> p t d", p=P), x[:, :, cols]).then_inc(stored, 16)
            sp.wait_ge(stored, 16 * 4)

        @block.gpsimd
        def _(pool):
            nc.gpsimd.memset(ones, 1.0).then_inc(memset_done, 1)
            nc.gpsimd.memset(cv[:, :, 0:1], 0.0).then_inc(memset_done, 1)
            nc.gpsimd.memset(cv[:, :, 257:258], 0.0).then_inc(memset_done, 1)
            for row, name in enumerate(("diff_q_norm_g_2", "diff_k_norm_g_2", "dil_q_norm_g_2", "dil_k_norm_g_2")):
                for half in range(2):
                    pool.dma_start(vec2[row:row + 1, half * DH:(half + 1) * DH], t[name]).then_inc(gain_loaded, 16)
            pool.dma_start(vec2[4:5, :], t["diff_sub_norm_g_2"]).then_inc(gain_loaded, 16)
            for n, name in enumerate(("lambda_q1_2", "lambda_k1_2", "lambda_q2_2", "lambda_k2_2")):
                pool.dma_start(lam_in[:, n, :], t[name][0].partition_broadcast(P)).then_inc(lam_loaded, 16)
            pool.wait_ge(gain_turned, 1)
            with nc.allow_non_contiguous_dma(reason="64 B rows of the small router"):
                pool.dma_start(wr, t["w_router"][0].rearrange("(k p) e -> p k e", p=P)).then_inc(router_loaded, 16)
            await_bank(pool, "head", head_u["seq23"], 1)
            pool.dma_start(gfin, t["g_final"].partition_broadcast(P)).then_inc(side_loaded, 16)
            await_bank(pool, "head", head_u["ya1"], 1)
            for row, q in ((gm_row, Q_GATE_M), (gf_row, Q_GATE_F)):
                pool.dma_start(row, t["b_ada"][0, q * P:q * P + D].partition_broadcast(P)).then_inc(gate_bias_loaded, 16)
            pool.wait_ge(slot_used, first_slot["w_o"] + WO)
            pool.dma_start(br, t["b_router"][0].partition_broadcast(P)).then_inc(router_loaded, 16)
            pool.dma_start(p_rows, t["p_2"][0, 0].rearrange("(t p) c -> p t c", p=P)).then_inc(side_loaded, 16)

            pool.wait_ge(xr_ready, 4)
            for tt in range(TT):
                nc.gpsimd.tensor_scalar(rows_tmp[:, tt, :], x[:, tt, :], stat[:, 1, 3, tt:tt + 1], None, ALU.mult).then_inc(pool_chain, 1)
            for tt in range(TT):
                pool.wait_ge(rows_hi_ready, tt + 1)
                pool.wait_ge(pool_chain, tt + 1)
                nc.gpsimd.tensor_tensor(rows_lo[:, tt, :], rows_tmp[:, tt, :], rows_hi[:, tt, :].bitcast(F32), ALU.subtract).then_inc(rows_ready, 1)
            nc.gpsimd.memset(zero, 0.0).then_inc(zero_ready, 1)

            def take(e, h):
                nc.gpsimd.tensor_copy(cur[h], xet[:, :, bass.ds(e * CAP, CAP)]).then_inc(cur_ready, 1)
                for tt in range(TT):
                    src = weigh_flat[:, tt, bass.ds(e * CAP, CAP)].unsqueeze(1).broadcast_to([P, 4, CAP])
                    nc.gpsimd.tensor_copy(gw_cur[h][:, tt], src).then_inc(cur_ready, 1)

            pool.wait_ge(xet_act, 4)
            pool.wait_ge(xet_dve, 4)
            pool.wait_ge(pick_ready, 4)
            take(0, 0)
            take(1, 1)
            with pool.Fori(0, NE // 2 - 1) as i:
                for h in range(2):
                    pool.wait_ge(slot_used, 2 * EXPERT_SLOTS * i + (HEAD_SLOTS + h * EXPERT_SLOTS + 16))
                    take(2 * i + (2 + h), h)
            pool.wait_ge(slot_used, FIRST_TAIL)
            pool.dma_start(bias, t["bias"].rearrange("(t p) h s -> p t h s", p=P)).then_inc(bias_loaded, 16)
            for s in pool_split:
                pool.wait_ge(hi_ready, split_no[s] + 1)
                nc.gpsimd.tensor_tensor(ring_r[place(s)[0]][:], ring[:, place(s)[0], :], ring_r[part_place[s]][:].bitcast(F32),
                                        ALU.subtract).then_inc(lo_pool_ready, 1)
                if s == pool_split[0]:
                    pool.wait_ge(lo_pool_ready, 1)
                    for i in range(2):
                        nc.gpsimd.memset(qz[i][DH:P, :, 0, :], 0.0).then_inc(memset_done, 1)
                        nc.gpsimd.memset(qz[i][0:DH, :, 1, :], 0.0).then_inc(memset_done, 1)
                    pool.wait_ge(memset_done, 7)

        @block.tensor
        def _(pe):
            mm = nc.tensor.matmul

            def end_first(ins):
                ins.then_inc(first_ready, 1)

            def end_second(ins, slots):
                if slots:
                    ins.then_inc(slot_used, slots)
                else:
                    ins.then_inc(second_ready, 1)

            def split_product(to, left, right, start, stop):
                mm(to, left[0], right[0], start=start, stop=False)
                mm(to, left[0], right[1], start=False, stop=False)
                return mm(to, left[1], right[0], start=False, stop=stop)

            def split_slot(s, **dims):
                if s in pool_split:
                    pe.wait_ge(lo_pool_ready, pool_split.index(s) + 1)
                else:
                    pe.wait_ge(lo_ready, len([n for n in split_no if n <= s and n not in pool_split]))
                return [shaped(ring_r[p][:], **dims) for p in (part_place[s], place(s)[0])]

            def transposed_product(s, u, act_parts):
                for j in range(2):
                    w = split_slot(s + j, k=KD, n=HALF)
                    for c in range(2):
                        for k in range(KD):
                            last = split_product(bank(2 * (u % 2) + j, c=2, s=SEQ)[:, c, :], [h[:, k, c * P:(c + 1) * P] for h in w],
                                                 [a[:, k, :] for a in act_parts], k == 0, k == KD - 1)
                    last.then_inc(slot_used, 1)

            def columns_rows(s, to, act_parts, await_k=None, before_last=None):
                w = split_slot(s, k=KD, n=HALF)
                for tt in range(TT):
                    for k in range(KD):
                        if await_k and tt == 0:
                            await_k(k)
                        last = split_product(to(tt), [a[:, k, tt * P:(tt + 1) * P] for a in act_parts], [h[:, k, :] for h in w],
                                             k == 0, k == KD - 1)
                    if before_last and tt == 0:
                        before_last(last)
                last.then_inc(slot_used, 1)

            def rows_product(s, u, await_k=None):
                for i in range(2):
                    columns_rows(s + i, lambda tt: bank(2 * (u % 2) + tt)[:, i * HALF:(i + 1) * HALF], (ht_hi, ht_lo),
                                 await_k if i == 0 else None, end_first if i else None)

            def begin(sems, u):
                for j in range(2):
                    pe.wait_ge(sems[2 * (u % 2) + j], u // 2 + 1)

            turned_norms = [0, 1, 3, 4]

            def turn_norm(n, first_bank):
                if n < 4:
                    pe.wait_ge(xr_ready, 2 * turned_norms.index(n) + 2)
                for q in range(4):
                    if n == 4 and q % 2 == 0:
                        pe.wait_ge(x_ready, 12 + q)
                    for c in range(2):
                        for tt in range(TT):
                            to = bank(first_bank + q, c=2, t=TT, m=P)[:, c, tt, :]
                            cols = slice((2 * q + c) * P, (2 * q + c + 1) * P)
                            if n == 0:
                                last = nc.tensor.transpose(to, xr[:, tt, cols], ident)
                            elif n == 4:
                                last = nc.tensor.transpose(to, x[:, tt, cols], ident)
                            else:
                                last = mm(to, (x if n == 1 else xg)[:, tt, cols], diag_r[:, tt, :], start=True, stop=True)
                    last.then_inc(norm_turned, 1)

            def modulation(b, k, to):
                s = first_slot[f"ada{b}_{k}"]
                arrived(pe, s)
                for g in range(4):
                    last = mm(psum[32 * g:32 * g + 32, to, :], c_rep[:, k, :], slot_in(s, g=4, n=512)[:, g, :],
                              start=(k == 0), stop=(k == KD - 1), tile_position=(0, 32 * g))
                last.then_inc(slot_used, 1)

            def turn_modulation(b, to):
                pe.wait_ge(mod_rows_ready, b + 1)
                for c in range(4):
                    last = nc.tensor.transpose(bank(to, c=4, m=P)[:, c, :], mod_rows[b][:, c * P:(c + 1) * P], ident)
                last.then_inc(mod_turned, 1)

            pe.wait_ge(tables_loaded, 16)
            pe.wait_ge(vec_loaded, 16 * VEC_DMAS)
            nc.tensor.transpose(psum[:, 7, 0:P], vec1, ident).then_inc(vec_turned, 1)
            pe.wait_ge(c_ready, 1)
            for k in range(KD):
                if k == 6:
                    turn_norm(0, 0)
                    pe.wait_ge(gain_loaded, 144)
                    nc.tensor.transpose(psum[:, 6, 0:5], vec2[0:5, :], ident[0:5, 0:5]).then_inc(gain_turned, 1)
                modulation(0, k, 4)
            turn_modulation(0, 5)

            for u, (name, slots) in enumerate(HEAD_UNITS):
                for bk in ADA_BEFORE.get(u, ()):
                    if bk == (1, 0):
                        pe.wait_ge(mod_ready, 1)
                    modulation(*bk, 3 + bk[0])
                if name == "fourier_in":
                    def norm_part(k):
                        pe.wait_ge(free[k // 2], 1)
                    rows_product(first_slot[name], u, norm_part)
                    continue
                begin(free, u)
                if name in IN_CHUNK:
                    transposed_product(first_slot[name], u, (ht_hi, ht_lo))
                elif name in ("seq01", "seq23"):
                    if name == "seq01":
                        pe.wait_ge(dft_loaded, 32)
                        await_read(pe, free, head_u["fourier_in"])
                    for j in range(2):
                        g = 2 * (name == "seq23") + j
                        for tt in range(TT):
                            last = mm(bank(2 * (u % 2) + j), u_rows[:, tt, g * P:(g + 1) * P], dfts[:, tt, :], start=(tt == 0), stop=(tt == 1))
                        end_first(last) if j == 0 else end_second(last, 0)
                elif name == "group":
                    await_read(pe, free, head_u["seq23"])
                    for j in range(2):
                        for c in range(2):
                            for part in range(2):
                                last = mm(bank(2 * (u % 2) + j, c=2, s=SEQ)[:, c, :], dftg[:, part * P:(part + 1) * P],
                                          ab[:, 2 * j + c, part * SEQ:(part + 1) * SEQ], start=(part == 0), stop=(part == 1))
                        end_first(last) if j == 0 else end_second(last, 0)
                elif name in ("ya0", "ya1"):
                    await_read(pe, free, head_u["group"])
                    w = split_slot(first_slot[name], k=FG, n=BANK)
                    for j in range(2):
                        for c in range(2):
                            at = slice((2 * j + c) * P, (2 * j + c + 1) * P)
                            for k in range(FG):
                                last = split_product(bank(2 * (u % 2) + j, c=2, s=SEQ)[:, c, :], [h[:, k, at] for h in w],
                                                     (fm_hi[:, k, :], fm_lo[:, k, :]), k == 0, k == FG - 1)
                        end_first(last) if j == 0 else end_second(last, slots)
                else:
                    pe.wait_ge(st_ready, 4)
                    transposed_product(first_slot[name], u, (st_hi, st_lo))
                    if name == "yb0":
                        pe.wait_ge(gain_ready, 1)
                        turn_modulation(1, 6)
                        turn_modulation(2, 7)
            pe.wait_ge(mod_ready, 2)
            for g, b, first in ((0, 1, 0), (1, 2, 2)):
                for n in range(2):
                    r = 32 * (first + n)
                    mm(bank(4 + 2 * g + n), ones[r:r + 1, :], mod_rows[b][r:r + 1, :], start=True, stop=True,
                       tile_position=(r, 0)).then_inc(gate_row_done, 1)
            begin(free, MIX_UNIT)
            begin(free, MIX_UNIT + 1)
            pe.wait_ge(z_ready, 4)
            for c in range(WO):
                columns_rows(first_slot["w_o"] + c, lambda tt: bank(2 * tt + c // 2)[:, c % 2 * HALF:(c % 2 + 1) * HALF], (ht_hi, ht_lo))

            pe.wait_ge(gate_row_ready, 4)
            turn_norm(1, 4)
            pe.wait_ge(router_loaded, 16)
            pe.wait_ge(norm_act, 2)
            pe.wait_ge(norm_dve, 2)
            await_read(pe, free, MIX_UNIT)
            await_read(pe, free, MIX_UNIT + 1)
            for tt in range(TT):
                for k in range(KD):
                    last = mm(psum[:, 0, tt * NE:(tt + 1) * NE], ht[:, k, tt * P:(tt + 1) * P], wr[:, k, :], start=(k == 0), stop=(k == KD - 1))
            last.then_inc(logits_done, 1)
            pe.wait_ge(prob_ready, 1)
            for tt in range(TT):
                last = nc.tensor.transpose(psum[0:NE, 1, tt * P:(tt + 1) * P], prob[:, tt, :], ident)
            last.then_inc(prob_turned, 1)
            pe.wait_ge(mask_ready, 1)
            for tt in range(TT):
                last = nc.tensor.transpose(psum[:, 2, tt * NE:(tt + 1) * NE], left_t[0:NE, tt * P:(tt + 1) * P], ident[0:NE, 0:NE])
            last.then_inc(mask_turned, 1)
            pe.wait_ge(sel_ready, 1)
            mm(psum[:, 3, 0:NE], before, sel[:, 0, :], start=True, stop=True)
            mm(psum[:, 3, NE:2 * NE], ones, sel[:, 0, :], start=True, stop=False)
            mm(psum[:, 3, NE:2 * NE], before, sel[:, 1, :], start=False, stop=True).then_inc(slots_done, 1)
            pe.wait_ge(pick_ready, 2)
            pe.wait_ge(rows_ready, 2)
            for k in range(KD):
                if k >= 4:
                    pe.wait_ge(xet_act if k % 2 == 0 else xet_dve, (k - 4) // 2 + 1)
                for tt in range(TT):
                    for n, rows in enumerate((rows_hi, rows_lo)):
                        last = mm(bank(4 + k % 4), rows[:, tt, k * P:(k + 1) * P], pick_flat[:, tt, :],
                                  start=(tt == 0 and n == 0), stop=(tt == 1 and n == 1))
                last.then_inc(gathered, 1)
            pe.wait_ge(xet_act, 4)
            pe.wait_ge(xet_dve, 4)
            pe.wait_ge(zero_ready, 1)
            for b in range(4):
                mm(bank(4 + b), zero[:, 0:P], zero, start=True, stop=True)

            with pe.Fori(0, NE // 2) as i:
                for h in range(2):
                    def slot_wait(j):
                        s = HEAD_SLOTS + h * EXPERT_SLOTS + j
                        p, n = place(s)
                        pe.wait_ge(loaded[p], 48 * i + 16 * n)
                        return s
                    pe.wait_ge(cur_ready, 6 * i + 3 * (h + 1))
                    for tt in range(TT):
                        last = nc.tensor.transpose(bank(2, t=4, m=P)[:, tt, :], gw_cur[h][:, tt].rearrange("p r s -> p (r s)"), ident)
                    last.then_inc(gw_turned, 1)
                    for b in range(2):
                        for k in range(KD):
                            s = slot_wait(8 * b + k)
                            for g in range(4):
                                last = mm(psum[32 * g:32 * g + 32, b, :], cur[h][:, k, :], slot_in(s, g=4, n=512)[:, g, :],
                                          start=(k == 0), stop=(k == KD - 1), tile_position=(0, 32 * g))
                            last.then_inc(slot_used, 1)
                    pe.wait_ge(act_ready, 2 * i + (h + 1))
                    for c in range(4):
                        last = nc.tensor.transpose(bank(0, c=4, m=P)[:, c, :], act_h[:, c * P:(c + 1) * P], ident)
                    last.then_inc(act_turned, 1)
                    pe.wait_ge(act_t_ready, 2 * i + (h + 1))
                    pe.wait_ge(gwt_ready, 2 * i + (h + 1))
                    for j in range(8):
                        s = slot_wait(16 + j)
                        w = slot_in(s, k=2, n=D)
                        for n in range(2):
                            for kk in range(2):
                                f = 2 * j + kk
                                q = f % 4
                                last = mm(psum[32 * q:32 * q + 32, 2 + n, :], act_t[:, f % 4, (f // 4) * CAP:(f // 4 + 1) * CAP],
                                          w[:, kk, n * BANK:(n + 1) * BANK], start=(f < 4), stop=(f >= 12), tile_position=(0, 32 * q))
                        last.then_inc(slot_used, 1)
                    pe.wait_ge(y_ready, 4 * i + 2 * (h + 1))
                    for tt in range(TT):
                        for n in range(2):
                            last = mm(bank(4 + 2 * tt + n), gwt[:, tt, :], y[:, n, :], start=False, stop=True, skip_group_check=True)
                    last.then_inc(scattered, 1)

            pe.wait_ge(side_loaded, 32)
            for c in range(2):
                for tt in range(TT):
                    last = nc.tensor.transpose(bank(3, c=2, t=TT, m=P)[:, c, tt, :], p_rows[:, tt, c * P:(c + 1) * P], ident)
            last.then_inc(pt_turned, 1)
            pe.wait_ge(pt_ready, 1)
            arrived(pe, first_slot["w_pp"])
            w = slot_in(first_slot["w_pp"], k=2, n=D)
            for tt in range(TT):
                for n in range(2):
                    for k in range(2):
                        last = mm(bank(2 * tt + n), pt[:, k, tt * P:(tt + 1) * P], w[:, k, n * BANK:(n + 1) * BANK], start=(k == 0), stop=(k == 1))
            last.then_inc(slot_used, 1)
            turn_norm(3, 4)

            def score_product(a):
                kind = ("diff", "dil")[a // 2]
                await_read(pe, tfree, tail_u["turn_q_" + kind])
                await_read(pe, tfree, tail_u["turn_k_" + kind])
                if a:
                    pe.wait_ge(scores_read, 4 * a)
                q, k = qz[a // 2], kt[a // 2]
                for j in range(4):
                    for c in range(2):
                        last = mm(bank(4 + j, c=2, s=SEQ)[:, c, :], q[:, j, c, (a % 2) * P:(a % 2 + 1) * P], k[:, j, :], start=True, stop=True)
                    last.then_inc(scores_done, 1)

            def out_product(first):
                for i in (first, first + 1):
                    pe.wait_ge(yt_ready, i + 1)
                    w = split_slot(first_slot["w_out"] + i, k=2, n=D)
                    for kk in range(2):
                        k = 2 * i + kk
                        for tt in range(TT):
                            for n in range(2):
                                last = split_product(bank(4 + 2 * tt + n), [a[:, k, tt * P:(tt + 1) * P] for a in (ht_hi, ht_lo)],
                                                     [h[:, kk, n * BANK:(n + 1) * BANK] for h in w], k == 0, k == KD - 1)
                    last.then_inc(slot_used, 1)

            for u, (name, slots) in enumerate(TAIL_UNITS):
                begin(tfree, u)
                if name in ("z0", "z1"):
                    transposed_product(first_slot[name], u, (ht_hi, ht_lo))
                elif name in IN2_CHUNK:
                    rows_product(first_slot[name], u, (lambda k: pe.wait_ge(norm_lo, k // 2 + 1)) if u == 0 else None)
                elif name.startswith(("turn_q", "turn_k")):
                    i = ("turn_q_diff", "turn_k_diff", "turn_q_dil", "turn_k_dil").index(name)
                    pe.wait_ge(qn_ready, 2 * i + 2)
                    for j in range(2):
                        for c in range(2):
                            for tt in range(TT):
                                last = nc.tensor.transpose(bank(2 * (u % 2) + j, c=2, t=TT, m=P)[:, c, tt, :],
                                                           qn[i][:, tt, (2 * j + c) * P:(2 * j + c + 1) * P], ident)
                        end_first(last) if j == 0 else end_second(last, 0)
                elif name.startswith("turn_w"):
                    a = int(name[6])
                    pe.wait_ge(w_ready, a + 1)
                    for j in range(2):
                        for c in range(2):
                            for kk in range(TT):
                                last = nc.tensor.transpose(bank(2 * (u % 2) + j, c=2, t=TT, m=P)[:, c, kk, :],
                                                           scores[a][:, 2 * (2 * j + c), kk * P:(kk + 1) * P], ident)
                        end_first(last) if j == 0 else end_second(last, 0)
                elif name.startswith("turn_e"):
                    a, part = int(name[6]), "ab".index(name[7])
                    pe.wait_ge(exps_done, 3 + a)
                    for j in range(2):
                        for c in range(2):
                            for kk in range(TT):
                                last = nc.tensor.transpose(bank(2 * (u % 2) + j, c=2, t=TT, m=P)[:, c, kk, :],
                                                           scores[a][:, 4 * part + 2 * j + c, kk * P:(kk + 1) * P], ident)
                        end_first(last) if j == 0 else end_second(last, 0)
                elif name == "pv_diff":
                    await_read(pe, tfree, tail_u["turn_w0"])
                    await_read(pe, tfree, tail_u["turn_w1"])
                    for tt in range(TT):
                        for hh in range(4):
                            for kk in range(TT):
                                last = mm(psum[:, 2 * (u % 2) + tt, hh * P:(hh + 1) * P], wt[:, 8 * tt + 2 * hh + kk, :], v[:, kk, hh * P:(hh + 1) * P],
                                          start=(kk == 0), stop=(kk == 1))
                        end_first(last) if tt == 0 else end_second(last, 0)
                elif name.startswith("pv_dil"):
                    await_read(pe, tfree, u - 2)
                    await_read(pe, tfree, u - 1)
                    for j in range(2):
                        for c in range(4):
                            hh = 4 * j + c
                            for kk in range(TT):
                                last = mm(psum[:, 2 * (u % 2) + j, c * DH:(c + 1) * DH], wt[:, 2 * hh + kk, :],
                                          v[:, kk, 512 + hh * DH:512 + (hh + 1) * DH], start=(kk == 0), stop=(kk == 1))
                        end_first(last) if j == 0 else end_second(last, 0)
                else:
                    i = int(name[-1])
                    if i == 0:
                        pe.wait_ge(cat_ready, 2)
                    else:
                        await_read(pe, tfree, tail_u["pv_dil0"])
                        await_read(pe, tfree, tail_u["pv_dil1"])
                    for j in range(2):
                        for c in range(2):
                            for tt in range(TT):
                                last = nc.tensor.transpose(bank(2 * (u % 2) + j, c=2, t=TT, m=P)[:, c, tt, :],
                                                           cat[:, tt, (4 * i + 2 * j + c) * P:(4 * i + 2 * j + c + 1) * P], ident)
                        end_first(last) if j == 0 else end_second(last, 0)
                if name in SCORES_AFTER:
                    score_product(SCORES_AFTER[name])
                if name == OUT_AFTER:
                    pe.wait_ge(scores_read, 16)
                    out_product(0)
            out_product(2)
            await_read(pe, tfree, len(TAIL_UNITS) - 2)
            await_read(pe, tfree, len(TAIL_UNITS) - 1)
            turn_norm(4, 0)
            pe.wait_ge(x_ready, 14)
            for c in range(4):
                columns_rows(first_slot["w_gate"] + c, lambda tt: bank(gate_bank(c, tt))[:, 0:HALF], (ht_hi, ht_lo),
                             (lambda k: pe.wait_ge(norm_lo, 4 + k // 2 + 1)) if c == 0 else None)

        @block.scalar
        def _(act):
            f = nc.scalar.activation
            count = [0]

            def link(ins):
                count[0] += 1
                ins.then_inc(act_chain, 1)
                act.wait_ge(act_chain, count[0])

            act.dma_start(small, t["small"]).then_inc(tables_loaded, 16)
            for at, src in vec_sources(t):
                act.dma_start(vec1[at:at + src.shape[0], :], src).then_inc(vec_loaded, 16)

            def squares(n, wait, rows=x):
                for tt in range(TT):
                    wait(tt)
                    f(xr[:, tt, :], rows[:, tt, :], ACT.Square, accum_out=stat[:, n, 0, tt:tt + 1]).then_inc(squared, 1)

            def load_root():
                f(spare_root, ones[:, 0:1], ACT.Sqrt)

            def half_squares(i, n, tt):
                cols = slice(n * BANK, (n + 1) * BANK)
                f(xr[:, tt, cols], x[:, tt, cols], ACT.Square, accum_out=half_sum[:, i, n, tt:tt + 1]).then_inc(squared, 1)

            def roots(n):
                act.wait_ge(mean_ready, n + 1)
                f(stat[:, n, 2, :], stat[:, n, 1, :], ACT.Sqrt).then_inc(root_ready, 1)

            def split_ahead(slots):
                for s in slots:
                    arrived(act, s)
                    if s in part_before:
                        act.wait_ge(slot_used, part_before[s] + 1)
                    f(ring_r[part_place[s]][:], ring[:, place(s)[0], :], ACT.Copy).then_inc(hi_ready, 1)

            def split_norm(n, first_bank, scale):
                for q in range(4):
                    act.wait_ge(norm_turned, 4 * n + q + 1)
                    for c in range(2):
                        k = 2 * q + c
                        ins = f(ht_hi[:, k, :], bank(first_bank + q, c=2, s=SEQ)[:, c, :], ACT.Copy, scale=scale[:, k:k + 1])
                    ins.then_inc(norm_hi, 1)

            def spread_norm(n, first_bank, scale, shift, sems=None):
                for q in (0, 2):
                    act.wait_ge(norm_turned, 4 * n + q + 1)
                    for c in range(2):
                        k = 2 * q + c
                        src = bank(first_bank + q, c=2, s=SEQ)[:, c, :]
                        if shift is None:
                            ins = f(ht[:, k, :], src, ACT.Copy, scale=scale[:, k:k + 1])
                        else:
                            ins = f(ht[:, k, :], src, ACT.Identity, scale=scale[:, k:k + 1], bias=shift[:, k:k + 1])
                    ins.then_inc(sems[q] if sems else norm_act, 1)

            act.wait_ge(vec_ready, 1)
            f(sig_c, col[:, C_C:C_C + KD], ACT.Sigmoid).then_inc(sig_c_ready, 1)
            squares(0, lambda tt: act.wait_ge(x_loaded, 16))
            roots(0)

            def modulation_rows(b, from_bank):
                act.wait_ge(slot_used, first_slot[f"ada{b}_{KD - 1}"] + 1)
                f(mod_rows[b], bank(from_bank), ACT.Copy).then_inc(mod_rows_ready, 1)

            modulation_rows(0, 4)
            act.wait_ge(mod_ready, 1)
            split_ahead([first_slot["fourier_in"]])
            for q in range(4):
                act.wait_ge(norm_spread, q + 1)
                f(ht_hi[:, 2 * q:2 * q + 2, :], norm_tmp[:, 2 * q:2 * q + 2, :], ACT.Copy).then_inc(norm_hi, 1)
            split_ahead([first_slot["fourier_in"] + 1])

            for u, (name, _) in enumerate(HEAD_UNITS):
                b = 2 * (u % 2)
                split_ahead(head_ahead[u])
                if name == "yb0":
                    modulation_rows(1, 4)
                    modulation_rows(2, 5)
                if name == "fourier_in":
                    await_bank(act, "head", u, 0)
                    f(u_rows[:, 0, :], bank(b), ACT.Copy).then_inc(free[b], 1)
                elif name in ("v0", "v1"):
                    await_bank(act, "head", u, 0)
                    f(vt[:, 0:2, :], bank(b, c=2, s=SEQ), ACT.Copy).then_inc(free[b], 1)
                elif name in ("seq01", "seq23"):
                    await_bank(act, "head", u, 0)
                    f(ab[:, 2 * (name == "seq23"), :], bank(b), ACT.Copy).then_inc(free[b], 1)
                elif name == "group":
                    for j in range(2):
                        await_bank(act, "head", u, j)
                        f(fm_hi[:, 2 * j:2 * j + 2, :], bank(b + j, c=2, s=SEQ), ACT.Copy).then_inc(fm_hi_ready, 1)
                elif name in ("b0", "b1"):
                    for j in range(2):
                        k = 4 * int(name[1]) + 2 * j
                        act.wait_ge(free[b + j], u // 2 + 2)
                        f(st_hi[:, k:k + 2, :], conv[:, 2 * j:2 * j + 2, :], ACT.Copy).then_inc(st_hi_ready, 1)
                elif name in ("yb0", "yb1"):
                    for j in range(2):
                        k = 4 * int(name[2]) + 2 * j
                        act.wait_ge(free[b + j], u // 2 + 2)
                        f(ht_hi[:, k:k + 2, :], ga[:, k:k + 2, :], ACT.Copy).then_inc(z_hi_ready, 1)
                elif name[:2] in ("ga", "gb"):
                    if name == "gb0":
                        await_read(act, free, head_u["c1"])
                    elif name == "gb1":
                        act.wait_ge(st_ready, 4)
                    for j in range(2):
                        await_bank(act, "head", u, j)
                        for c in range(2):
                            k = 4 * int(name[2]) + 2 * j + c
                            at = C_BGATE + (0 if name[:2] == "ga" else KD) + k
                            gate = ga[:, k, :] if name[:2] == "ga" else gb[k // 4][:, k % 4, :]
                            ins = f(gate, bank(b + j, c=2, s=SEQ)[:, c, :], ACT.Sigmoid, bias=col[:, at:at + 1])
                        ins.then_inc(free[b + j], 1)
            split_ahead([first_slot["w_o"] + 2, first_slot["w_o"] + 3])
            load_root()
            for n in range(2):
                for tt in range(TT):
                    act.wait_ge(x_ready, 2 * n + tt + 1)
                    half_squares(0, n, tt)
            roots(1)
            spread_norm(1, 4, mod_a[:, KD:2 * KD], mod_t[:, Q_SHIFT_F:])
            for tt in range(TT):
                f(rows_hi[:, tt, :], x[:, tt, :], ACT.Copy, scale=stat[:, 1, 3, tt:tt + 1]).then_inc(rows_hi_ready, 1)
            act.wait_ge(soft_in, 1)
            f(prob, logit, ACT.Exp).then_inc(exp_ready, 1)
            act.wait_ge(lam_sums, 2)
            f(lam_s[:, 2:4], lam_s[:, 0:2], ACT.Exp).then_inc(lam_exps, 1)
            for k in range(0, KD, 2):
                act.wait_ge(gathered, k + 1)
                f(xet[:, k, :], bank(4 + k % 4), ACT.Identity, scale=mod_a[:, KD + k:KD + k + 1],
                  bias=mod_t[:, Q_SHIFT_F + k:Q_SHIFT_F + k + 1]).then_inc(xet_act, 1)

            with act.Fori(0, NE // 2) as i:
                for h in range(2):
                    act.wait_ge(gw_turned, 2 * i + (h + 1))
                    f(gwt, bank(2, t=4, m=P)[:, 0:TT, :], ACT.Copy).then_inc(gwt_ready, 1)
                    act.wait_ge(slot_used, 2 * EXPERT_SLOTS * i + (HEAD_SLOTS + h * EXPERT_SLOTS + 8))
                    f(sig_a, bank(0), ACT.Sigmoid).then_inc(sig_ready, 1)
                    act.wait_ge(act_turned, 2 * i + (h + 1))
                    f(act_t, bank(0, c=4, m=P), ACT.Copy).then_inc(act_t_ready, 1)

            split_ahead([first_slot["q_diff"]])
            act.wait_ge(pt_turned, 1)
            f(pt, bank(3, c=2, s=SEQ), ACT.Copy).then_inc(pt_ready, 1)
            load_root()
            squares(2, lambda tt: act.wait_ge(x_ready, 4 + 2 * tt + 2))
            roots(2)
            squares(3, lambda tt: act.wait_ge(x_ready, 8 + tt + 1), xg)
            roots(3)
            for b in (0, 2):
                act.wait_ge(slot_used, first_slot["w_pp"] + 1)
                f(pp[:, b // 2, 0:BANK], bank(b), ACT.Copy).then_inc(tfree[b], 1)
            split_ahead([first_slot["q_diff"] + 1])
            split_norm(2, 4, col[:, C_MIX2:C_MIX2 + KD])

            def exponentials(a):
                act.wait_ge(max_ready, a + 1)
                s = scores[a % 2]
                for hh in range(8):
                    ins = f(s[:, hh, :], s[:, hh, :], ACT.Exp, bias=soft[:, a, 0, hh:hh + 1], accum_out=soft[:, a, 1, hh:hh + 1])
                ins.then_inc(exps_done, 1)

            for u, (name, _) in enumerate(TAIL_UNITS):
                b = 2 * (u % 2)
                split_ahead(tail_ahead.get(u, ()))
                if name in ("q_diff", "k_diff", "q_dil", "k_dil"):
                    i = ("q_diff", "k_diff", "q_dil", "k_dil").index(name)
                    for tt in range(TT):
                        await_bank(act, "tail", u, tt)
                        if i:
                            act.wait_ge(qk_mean, i)
                        f(sqt[:, tt, :], bank(b + tt), ACT.Square).then_inc(qk_squared, 1)
                        f(qn[i][:, tt, :], bank(b + tt), ACT.Copy).then_inc(tfree[b + tt], 1)
                    act.wait_ge(qk_mean, i + 1)
                    f(head_stat[:, 2, :], head_stat[:, 1, :], ACT.Sqrt).then_inc(qk_root, 1)
                elif name.startswith("turn_q"):
                    i = int(name == "turn_q_dil")
                    act.wait_ge(memset_done, 7)
                    await_bank(act, "tail", u, 0)
                    for c in range(2):
                        r = slice(c * DH, (c + 1) * DH)
                        ins = f(qz[i][r, 0:2, c, :], bank(b, c=2, s=SEQ)[r], ACT.Copy, scale=gain[r, 2 * i:2 * i + 1])
                    ins.then_inc(tfree[b], 1)
                elif name.startswith("turn_k"):
                    i = int(name == "turn_k_dil")
                    await_bank(act, "tail", u, 0)
                    f(kt[i][:, 0:2, :], bank(b, c=2, s=SEQ), ACT.Copy, scale=gain[:, 2 * i + 1:2 * i + 2]).then_inc(tfree[b], 1)
                elif name in ("v_diff", "v_dil"):
                    at = 512 * (name == "v_dil")
                    await_bank(act, "tail", u, 0)
                    f(v[:, 0, at:at + 512], bank(b), ACT.Copy).then_inc(tfree[b], 1)
                elif name in ("z0", "z1"):
                    n = int(name[1])
                    if n:
                        await_read(act, tfree, tail_u["z0"])
                    for j in range(2):
                        await_bank(act, "tail", u, j)
                        f(sgz[:, 2 * j:2 * j + 2, :], bank(b + j, c=2, s=SEQ), ACT.Sigmoid).then_inc(sgz_ready, 1)
                elif name.startswith(("turn_w", "turn_e")):
                    i = {"turn_w0": 0, "turn_w1": 8, "turn_e0a": 0, "turn_e0b": 8, "turn_e1a": 0, "turn_e1b": 8}[name]
                    await_bank(act, "tail", u, 0)
                    f(wt[:, i:i + 4, :], bank(b, i=4, m=P), ACT.Copy).then_inc(tfree[b], 1)
                elif name == "pv_diff":
                    for tt in range(TT):
                        await_bank(act, "tail", u, tt)
                        f(sqt[:, tt, :], bank(b + tt), ACT.Square).then_inc(qk_squared, 1)
                        f(cat[:, tt, 0:512], bank(b + tt), ACT.Copy).then_inc(tfree[b + tt], 1)
                    act.wait_ge(qk_mean, 5)
                    f(head_stat[:, 2, 0:8], head_stat[:, 1, 0:8], ACT.Sqrt).then_inc(qk_root, 1)
                elif name.startswith("turn_cat"):
                    for j in range(2):
                        k = 4 * int(name[-1]) + 2 * j
                        act.wait_ge(tfree[b + j], u // 2 + 2)
                        f(ht_hi[:, k:k + 2, :], szt[:, k:k + 2, :], ACT.Copy).then_inc(yt_hi_ready, 1)
                split_ahead(ahead_late.get(name, ()))
                if name in EXPS_AFTER:
                    exponentials(EXPS_AFTER[name])

            split_ahead([first_slot["w_out"] + 3, first_slot["w_gate"], first_slot["w_gate"] + 1])
            load_root()
            split_norm(3, 0, col[:, C_PLE:C_PLE + KD])
            for n in range(2):
                for tt in range(TT):
                    half_squares(1, n, tt)
            roots(4)
            act.wait_ge(scale_ready, 5)
            split_ahead([first_slot["w_gate"] + 2, first_slot["w_gate"] + 3])
            for c in range(4):
                act.wait_ge(slot_used, first_slot["w_gate"] + c + 1)
                for tt in range(TT):
                    f(gt[:, tt, c * HALF:(c + 1) * HALF], bank(gate_bank(c, tt))[:, 0:HALF], ACT.Sigmoid,
                      scale=stat[:, 4, 3, tt:tt + 1]).then_inc(gate_sig, 1)

        @block.vector
        def _(dve):
            count = [0]
            V = nc.vector

            def link(ins):
                count[0] += 1
                ins.then_inc(dve_chain, 1)
                dve.wait_ge(dve_chain, count[0])

            sums_before = [0, 2, 6, 8, 10]

            def norm_rows(n, halves=None):
                dve.wait_ge(squared, sums_before[n] + (2 if halves is None else 4))
                if halves is not None:
                    link(V.tensor_tensor(stat[:, n, 0, :], half_sum[:, halves, 0, :], half_sum[:, halves, 1, :], ALU.add))
                V.tensor_scalar(stat[:, n, 1, :], stat[:, n, 0, :], 1.0 / D, EPS, ALU.mult, ALU.add).then_inc(mean_ready, 1)
                dve.wait_ge(root_ready, n + 1)
                V.reciprocal(stat[:, n, 3, :], stat[:, n, 2, :]).then_inc(scale_ready, 1)
                dve.wait_ge(scale_ready, n + 1)

            def norm_diagonal(n):
                for tt in range(TT):
                    V.tensor_scalar(diag_r[:, tt, :], ident, stat[:, n, 3, tt:tt + 1], None, ALU.mult).then_inc(xr_ready, 1)

            def spread_norm(n, first_bank, scale, shift, sems=None):
                for q in (1, 3):
                    dve.wait_ge(norm_turned, 4 * n + q + 1)
                    for c in range(2):
                        k = 2 * q + c
                        src = bank(first_bank + q, c=2, s=SEQ)[:, c, :]
                        if shift is None:
                            ins = V.tensor_scalar(ht[:, k, :], src, scale[:, k:k + 1], None, ALU.mult)
                        else:
                            ins = V.tensor_scalar(ht[:, k, :], src, scale[:, k:k + 1], shift[:, k:k + 1], ALU.mult, ALU.add)
                    ins.then_inc(sems[q] if sems else norm_dve, 1)

            def split_ahead(slots):
                for s in slots:
                    if s in pool_split:
                        continue
                    dve.wait_ge(hi_ready, split_no[s] + 1)
                    V.tensor_tensor(ring_r[place(s)[0]][:], ring[:, place(s)[0], :], ring_r[part_place[s]][:].bitcast(F32),
                                    ALU.subtract).then_inc(lo_ready, 1)

            def rest(to, whole, hi, ready):
                V.tensor_tensor(to, whole, hi.bitcast(F32), ALU.subtract).then_inc(ready, 1)

            def split_norm(first_bank, scale, at):
                for q in range(4):
                    dve.wait_ge(norm_hi, at + q + 1)
                    for c in range(2):
                        k = 2 * q + c
                        ins = V.scalar_tensor_tensor(ht_lo[:, k, :], bank(first_bank + q, c=2, s=SEQ)[:, c, :], scale[:, k:k + 1],
                                                     ht_hi[:, k, :].bitcast(F32), ALU.mult, ALU.subtract)
                    ins.then_inc(norm_lo, 1)

            def modulation_columns(b, from_bank):
                dve.wait_ge(mod_turned, b + 1)
                src = bank(from_bank, c=4, g=4, r=32)[:, :, :, 0].rearrange("p c g -> p g c")
                at = slice(16 * b, 16 * b + 16)
                link(V.tensor_tensor(shaped(mod_t[:, at], g=4, c=4), src, shaped(col[:, C_BADA + 16 * b:C_BADA + 16 * b + 16], g=4, c=4), ALU.add))

            dve.wait_ge(vec_turned, 1)
            V.tensor_copy(col, psum[:, 7, 0:P]).then_inc(vec_ready, 1)
            dve.wait_ge(vec_ready, 1)
            dve.wait_ge(sig_c_ready, 1)
            link(V.tensor_tensor(c_act, col[:, C_C:C_C + KD], sig_c, ALU.mult))
            V.tensor_copy(c_rep, c_act.unsqueeze(2).broadcast_to([P, KD, 32])).then_inc(c_ready, 1)
            dve.wait_ge(x_loaded, 16)
            norm_rows(0)
            for tt in range(TT):
                V.tensor_scalar(xr[:, tt, :], x[:, tt, :], stat[:, 0, 3, tt:tt + 1], None, ALU.mult).then_inc(xr_ready, 1)
            dve.wait_ge(gain_turned, 1)
            V.tensor_copy(gain[:, 0:5], psum[:, 6, 0:5]).then_inc(gain_ready, 1)
            dve.wait_ge(gain_ready, 1)
            V.tensor_scalar(sub_gain, gain[:, 4:5], 1.0 - LAM_INIT, None, ALU.mult)
            modulation_columns(0, 5)
            V.scalar_tensor_tensor(mod_a[:, 0:KD], mod_t[:, Q_SCALE_M:Q_SCALE_M + KD], 1.0, col[:, C_GMIX:C_GMIX + KD],
                                   ALU.add, ALU.mult).then_inc(mod_ready, 1)
            dve.wait_ge(mod_ready, 1)
            for k in range(KD):
                if k % 2 == 0:
                    dve.wait_ge(norm_turned, k // 2 + 1)
                ins = V.tensor_scalar(norm_tmp[:, k, :], bank(k // 2, c=2, s=SEQ)[:, k % 2, :], mod_a[:, k:k + 1],
                                      mod_t[:, Q_SHIFT_M + k:Q_SHIFT_M + k + 1], ALU.mult, ALU.add)
                if k % 2:
                    ins.then_inc(norm_spread, 1)
            split_ahead([first_slot["fourier_in"]])
            for q in range(4):
                dve.wait_ge(norm_hi, q + 1)
                rest(ht_lo[:, 2 * q:2 * q + 2, :], norm_tmp[:, 2 * q:2 * q + 2, :], ht_hi[:, 2 * q:2 * q + 2, :], free[q])
            split_ahead([first_slot["fourier_in"] + 1])

            for u, (name, _) in enumerate(HEAD_UNITS):
                b = 2 * (u % 2)
                split_ahead(head_ahead[u])
                if name == "fourier_in":
                    await_bank(dve, "head", u, 1)
                    V.tensor_copy(u_rows[:, 1, :], bank(b + 1)).then_inc(free[b + 1], 1)
                elif name in ("v0", "v1"):
                    await_bank(dve, "head", u, 1)
                    V.tensor_copy(vt[:, 2:4, :], bank(b + 1, c=2, s=SEQ)).then_inc(free[b + 1], 1)
                elif name in ("seq01", "seq23"):
                    await_bank(dve, "head", u, 1)
                    V.tensor_copy(ab[:, 2 * (name == "seq23") + 1, :], bank(b + 1)).then_inc(free[b + 1], 1)
                elif name == "group":
                    for j in range(2):
                        dve.wait_ge(fm_hi_ready, j + 1)
                        rest(fm_lo[:, 2 * j:2 * j + 2, :], bank(b + j, c=2, s=SEQ), fm_hi[:, 2 * j:2 * j + 2, :], free[b + j])
                elif name in ("c0", "c1"):
                    await_read(dve, free, head_u["v" + name[1]])
                    dve.wait_ge(memset_done, 3)
                    for j in range(2):
                        await_bank(dve, "head", u, j)
                        V.tensor_tensor(cv[:, 2 * j:2 * j + 2, 1:SEQ + 1], bank(b + j, c=2, s=SEQ), vt[:, 2 * j:2 * j + 2, :],
                                        ALU.mult).then_inc(free[b + j], 1)
                    await_read(dve, free, u)
                    for tap in range(3):
                        for c in range(4):
                            w = C_CONV + tap * KD + 4 * int(name[1]) + c
                            src = cv[:, c, tap:tap + SEQ]
                            if tap == 0:
                                ins = V.tensor_scalar(conv[:, c, :], src, col[:, w:w + 1], None, ALU.mult)
                            else:
                                ins = V.scalar_tensor_tensor(conv[:, c, :], src, col[:, w:w + 1], conv[:, c, :], ALU.mult, ALU.add)
                        link(ins)
                elif name in ("b0", "b1"):
                    for j in range(2):
                        await_bank(dve, "head", u, j)
                        V.tensor_tensor(conv[:, 2 * j:2 * j + 2, :], bank(b + j, c=2, s=SEQ), conv[:, 2 * j:2 * j + 2, :],
                                        ALU.mult).then_inc(free[b + j], 1)
                    for j in range(2):
                        k = 4 * int(name[1]) + 2 * j
                        dve.wait_ge(st_hi_ready, k // 2 + 1)
                        rest(st_lo[:, k:k + 2, :], conv[:, 2 * j:2 * j + 2, :], st_hi[:, k:k + 2, :], st_ready)
                elif name in ("ya0", "ya1"):
                    await_read(dve, free, head_u["ga" + name[2]])
                    for j in range(2):
                        await_bank(dve, "head", u, j)
                        k = 4 * int(name[2]) + 2 * j
                        V.tensor_tensor(ga[:, k:k + 2, :], bank(b + j, c=2, s=SEQ), ga[:, k:k + 2, :], ALU.mult).then_inc(free[b + j], 1)
                elif name in ("yb0", "yb1"):
                    await_read(dve, free, head_u["gb" + name[2]])
                    await_read(dve, free, head_u["ya" + name[2]])
                    for j in range(2):
                        await_bank(dve, "head", u, j)
                        k = 4 * int(name[2]) + 2 * j
                        gate = gb[int(name[2])][:, 2 * j:2 * j + 2, :]
                        link(V.tensor_tensor(gate, bank(b + j, c=2, s=SEQ), gate, ALU.mult))
                        V.tensor_tensor(ga[:, k:k + 2, :], ga[:, k:k + 2, :], gate, ALU.add).then_inc(free[b + j], 1)
                    for j in range(2):
                        k = 4 * int(name[2]) + 2 * j
                        dve.wait_ge(z_hi_ready, k // 2 + 1)
                        rest(ht_lo[:, k:k + 2, :], ga[:, k:k + 2, :], ht_hi[:, k:k + 2, :], z_ready)
                    if name == "yb0":
                        modulation_columns(1, 6)
                        modulation_columns(2, 7)
                        V.scalar_tensor_tensor(mod_a[:, KD:2 * KD], mod_t[:, Q_SCALE_F:Q_SCALE_F + KD], 1.0, col[:, C_GMOE:C_GMOE + KD],
                                               ALU.add, ALU.mult).then_inc(mod_ready, 1)
            split_ahead([first_slot["w_o"] + 2, first_slot["w_o"] + 3])
            dve.wait_ge(lam_loaded, 64)
            for n in range(2):
                link(V.tensor_tensor(lam_in[:, 2 * n, :], lam_in[:, 2 * n, :], lam_in[:, 2 * n + 1, :], ALU.mult))
                V.tensor_reduce(lam_s[:, n:n + 1], lam_in[:, 2 * n, :], AX.X, ALU.add).then_inc(lam_sums, 1)
            dve.wait_ge(gate_bias_loaded, 32)
            for g, row in ((0, gm_row), (1, gf_row)):
                for n in range(2):
                    dve.wait_ge(gate_row_done, 2 * g + n + 1)
                    cols = slice(n * BANK, (n + 1) * BANK)
                    V.tensor_tensor(row[:, cols], bank(4 + 2 * g + n), row[:, cols], ALU.add).then_inc(gate_row_ready, 1)
            dve.wait_ge(gate_row_ready, 2)
            for n in range(2):
                dve.wait_ge(slot_used, first_slot["w_o"] + 2 * n + 2)
                for tt in range(TT):
                    b = 2 * tt + n
                    cols = slice(n * BANK, (n + 1) * BANK)
                    if n:
                        dve.wait_ge(x_ready, tt + 1)
                    V.tensor_tensor(mix_tmp[:, tt, :], bank(b), gm_row[:, cols], ALU.mult).then_inc(free[b], 1)
                    dve.wait_ge(free[b], MIX_UNIT // 2 + 2)
                    V.tensor_tensor(x[:, tt, cols], x[:, tt, cols], mix_tmp[:, tt, :], ALU.add).then_inc(x_ready, 1)
            dve.wait_ge(x_ready, 4)
            norm_rows(1, halves=0)
            norm_diagonal(1)
            dve.wait_ge(mod_ready, 2)
            spread_norm(1, 4, mod_a[:, KD:2 * KD], mod_t[:, Q_SHIFT_F:])

            dve.wait_ge(logits_done, 1)
            dve.wait_ge(router_loaded, 32)
            link(V.tensor_tensor(logit, bank(0)[:, 0:32].rearrange("p (t e) -> p t e", t=TT), br.unsqueeze(1).broadcast_to([P, TT, NE]), ALU.add))
            link(V.tensor_reduce(route[:, 0, :], logit, AX.X, ALU.max))
            V.tensor_tensor(logit, logit, route[:, 0, :].unsqueeze(2).broadcast_to([P, TT, NE]), ALU.subtract).then_inc(soft_in, 1)
            dve.wait_ge(exp_ready, 1)
            link(V.tensor_reduce(route[:, 1, :], prob, AX.X, ALU.add))
            link(V.reciprocal(route[:, 2, :], route[:, 1, :]))
            V.tensor_tensor(prob, prob, route[:, 2, :].unsqueeze(2).broadcast_to([P, TT, NE]), ALU.mult).then_inc(prob_ready, 1)
            dve.wait_ge(prob_turned, 1)
            link(V.tensor_copy(left_t[0:NE, :], psum[0:NE, 1, 0:SEQ]))
            for _ in range(CAP // 8):
                link(V.max(top8[0:NE, :], left_t[0:NE, :]))
                link(V.match_replace(left_t[0:NE, :], top8[0:NE, :], left_t[0:NE, :], -1.0))
            V.tensor_scalar(left_t[0:NE, :], left_t[0:NE, :], 0.0, None, ALU.is_lt).then_inc(mask_ready, 1)
            dve.wait_ge(mask_turned, 1)
            V.tensor_copy(sel, bank(2)[:, 0:32].rearrange("p (t e) -> p t e", t=TT)).then_inc(sel_ready, 1)
            dve.wait_ge(sel_ready, 1)
            dve.wait_ge(slots_done, 1)
            link(V.scalar_tensor_tensor(slot_of, sel, -UNPICKED, bank(3)[:, 0:32].rearrange("p (t e) -> p t e", t=TT), ALU.mult, ALU.add))
            for tt in range(TT):
                V.tensor_tensor(pick[:, tt], slot_of[:, tt, :].unsqueeze(2).broadcast_to([P, NE, CAP]),
                                slot_no.unsqueeze(1).broadcast_to([P, NE, CAP]), ALU.is_equal).then_inc(pick_ready, 1)
            dve.wait_ge(prob_ready, 1)
            dve.wait_ge(pick_ready, 2)
            for tt in range(TT):
                V.tensor_tensor(weigh[:, tt], pick[:, tt].bitcast(F32), prob[:, tt, :].unsqueeze(2).broadcast_to([P, NE, CAP]), ALU.mult).then_inc(pick_ready, 1)
            for k in range(1, KD, 2):
                dve.wait_ge(gathered, k + 1)
                V.tensor_scalar(xet[:, k, :], bank(4 + k % 4), mod_a[:, KD + k:KD + k + 1], mod_t[:, Q_SHIFT_F + k:Q_SHIFT_F + k + 1],
                                ALU.mult, ALU.add).then_inc(xet_dve, 1)

            dve.wait_ge(gate_row_ready, 4)
            with dve.Fori(0, NE // 2) as i:
                for h in range(2):
                    dve.wait_ge(sig_ready, 2 * i + (h + 1))
                    V.tensor_tensor(sig_a, bank(0), sig_a, ALU.mult).then_inc(gated, 1)
                    dve.wait_ge(gated, 2 * i + (h + 1))
                    dve.wait_ge(slot_used, 2 * EXPERT_SLOTS * i + (HEAD_SLOTS + h * EXPERT_SLOTS + 16))
                    V.tensor_tensor(act_h, bank(1), sig_a, ALU.mult).then_inc(act_ready, 1)
                    dve.wait_ge(slot_used, 2 * EXPERT_SLOTS * i + (HEAD_SLOTS + (h + 1) * EXPERT_SLOTS))
                    for n in range(2):
                        V.tensor_tensor(y[:, n, :], bank(2 + n), gf_row[:, n * BANK:(n + 1) * BANK], ALU.mult).then_inc(y_ready, 1)

            split_ahead([first_slot["q_diff"]])
            dve.wait_ge(scattered, NE)
            for tt in range(TT):
                for n in range(2):
                    cols = slice(n * BANK, (n + 1) * BANK)
                    V.tensor_tensor(x[:, tt, cols], x[:, tt, cols], bank(4 + 2 * tt + n), ALU.add).then_inc(x_ready, 1)
            for tt in range(TT):
                dve.wait_ge(x_ready, 4 + 2 * tt + 2)
                V.tensor_tensor(xg[:, tt, :], x[:, tt, :], gfin, ALU.mult).then_inc(x_ready, 1)
            norm_rows(2)
            dve.wait_ge(squared, sums_before[3] + 2)
            first = stat[:, 2, 3, :]
            link(V.tensor_tensor(stat[:, 3, 0, :], stat[:, 3, 0, :], first, ALU.mult))
            link(V.tensor_tensor(stat[:, 3, 0, :], stat[:, 3, 0, :], first, ALU.mult))
            norm_rows(3)
            link(V.tensor_tensor(stat[:, 3, 3, :], stat[:, 3, 3, :], first, ALU.mult))
            norm_diagonal(3)
            for tt in range(TT):
                ins = V.tensor_scalar(x[:, tt, :], xg[:, tt, :], stat[:, 2, 3, tt:tt + 1], None, ALU.mult)
            link(ins)
            for b in (1, 3):
                dve.wait_ge(slot_used, first_slot["w_pp"] + 1)
                V.tensor_copy(pp[:, b // 2, BANK:2 * BANK], bank(b)).then_inc(tfree[b], 1)
            dve.wait_ge(lam_exps, 1)
            link(V.tensor_tensor(lam_s[:, 4:5], lam_s[:, 3:4], lam_s[:, 2:3], ALU.subtract))
            link(V.tensor_scalar(lam_s[:, 5:6], lam_s[:, 4:5], LAM_INIT, None, ALU.subtract))
            split_ahead([first_slot["q_diff"] + 1])
            split_norm(4, col[:, C_MIX2:C_MIX2 + KD], 4)

            def head_roots(n, width, heads, target):
                dve.wait_ge(qk_squared, 2 * n + 2)
                nh = TT * heads
                for tt in range(TT):
                    ins = V.tensor_reduce(head_stat[:, 0, tt * heads:(tt + 1) * heads], shaped(sqt[:, tt, :], h=heads, e=width), AX.X, ALU.add)
                link(ins)
                V.tensor_scalar(head_stat[:, 1, 0:nh], head_stat[:, 0, 0:nh], 1.0 / width, EPS, ALU.mult, ALU.add).then_inc(qk_mean, 1)
                dve.wait_ge(qk_root, n + 1)
                link(V.reciprocal(head_stat[:, 3, 0:nh], head_stat[:, 2, 0:nh]))
                for tt in range(TT):
                    rows = target(tt).rearrange("p (h e) -> p h e", h=heads)
                    r = head_stat[:, 3, tt * heads:(tt + 1) * heads].unsqueeze(2).broadcast_to([P, heads, width])
                    V.tensor_tensor(rows, rows, r, ALU.mult).then_inc(qn_ready if n < 4 else cat_ready, 1)

            def score_max(a):
                s = scores[a % 2]
                dve.wait_ge(bias_loaded, 16)
                for j in range(4):
                    dve.wait_ge(scores_done, 4 * a + j + 1)
                    if a < 2:
                        pos = bias[:, a % 2, j, :].unsqueeze(1).broadcast_to([P, 2, SEQ])
                    else:
                        pos = bias[:, a % 2, 4 + 2 * j:6 + 2 * j, :]
                    V.scalar_tensor_tensor(s[:, 2 * j:2 * j + 2, :], bank(4 + j, c=2, s=SEQ), SCALE, pos, ALU.mult, ALU.add).then_inc(scores_read, 1)
                dve.wait_ge(scores_read, 4 * a + 4)
                V.tensor_reduce(soft[:, a, 0, :], s, AX.X, ALU.max, negate=True).then_inc(max_ready, 1)

            def diff_weights(a):
                s = scores[a]
                dve.wait_ge(exps_done, a + 1)
                link(V.reciprocal(soft[:, a, 2, :], soft[:, a, 1, :]))
                link(V.tensor_scalar(soft[:, a, 3, :], soft[:, a, 2, :], lam_s[:, 5:6], None, ALU.mult))
                for hh in range(4):
                    ins = V.tensor_scalar(s[:, 2 * hh, :], s[:, 2 * hh, :], soft[:, a, 2, 2 * hh:2 * hh + 1], None, ALU.mult)
                link(ins)
                for hh in range(4):
                    ins = V.scalar_tensor_tensor(s[:, 2 * hh, :], s[:, 2 * hh + 1, :], soft[:, a, 3, 2 * hh + 1:2 * hh + 2], s[:, 2 * hh, :],
                                                 ALU.mult, ALU.add)
                ins.then_inc(w_ready, 1)

            for u, (name, _) in enumerate(TAIL_UNITS):
                b = 2 * (u % 2)
                split_ahead(tail_ahead.get(u, ()))
                if name in ("q_diff", "k_diff", "q_dil", "k_dil"):
                    i = ("q_diff", "k_diff", "q_dil", "k_dil").index(name)
                    await_read(dve, tfree, u)
                    head_roots(i, DH, 8, lambda tt: qn[i][:, tt, :])
                elif name.startswith("turn_q"):
                    i = int(name == "turn_q_dil")
                    dve.wait_ge(memset_done, 7)
                    await_bank(dve, "tail", u, 1)
                    for c in range(2):
                        r = slice(c * DH, (c + 1) * DH)
                        ins = V.tensor_scalar(qz[i][r, 2:4, c, :], bank(b + 1, c=2, s=SEQ)[r], gain[r, 2 * i:2 * i + 1], None, ALU.mult)
                    ins.then_inc(tfree[b + 1], 1)
                elif name.startswith("turn_k"):
                    i = int(name == "turn_k_dil")
                    await_bank(dve, "tail", u, 1)
                    V.tensor_scalar(kt[i][:, 2:4, :], bank(b + 1, c=2, s=SEQ), gain[:, 2 * i + 1:2 * i + 2], None, ALU.mult).then_inc(tfree[b + 1], 1)
                elif name in ("v_diff", "v_dil"):
                    at = 512 * (name == "v_dil")
                    await_bank(dve, "tail", u, 1)
                    V.tensor_copy(v[:, 1, at:at + 512], bank(b + 1)).then_inc(tfree[b + 1], 1)
                elif name in ("z0", "z1"):
                    n = int(name[1])
                    for j in range(2):
                        dve.wait_ge(sgz_ready, 2 * n + j + 1)
                        k = 4 * n + 2 * j
                        V.tensor_tensor(szt[:, k:k + 2, :], bank(b + j, c=2, s=SEQ), sgz[:, 2 * j:2 * j + 2, :], ALU.mult).then_inc(tfree[b + j], 1)
                elif name.startswith(("turn_w", "turn_e")):
                    i = {"turn_w0": 4, "turn_w1": 12, "turn_e0a": 4, "turn_e0b": 12, "turn_e1a": 4, "turn_e1b": 12}[name]
                    await_bank(dve, "tail", u, 1)
                    V.tensor_copy(wt[:, i:i + 4, :], bank(b + 1, i=4, m=P)).then_inc(tfree[b + 1], 1)
                elif name == "pv_diff":
                    await_read(dve, tfree, u)
                    head_roots(4, P, 4, lambda tt: cat[:, tt, 0:512])
                elif name.startswith("pv_dil"):
                    tt = int(name[6])
                    dve.wait_ge(exps_done, 3 + tt)
                    link(V.reciprocal(soft[:, 2 + tt, 2, :], soft[:, 2 + tt, 1, :]))
                    for j in range(2):
                        await_bank(dve, "tail", u, j)
                        r = soft[:, 2 + tt, 2, 4 * j:4 * j + 4].unsqueeze(2).broadcast_to([P, 4, DH])
                        V.tensor_tensor(cat[:, tt, 512 + 256 * j:768 + 256 * j].rearrange("p (h e) -> p h e", h=4),
                                        bank(b + j)[:, 0:256].rearrange("p (h e) -> p h e", h=4), r, ALU.mult).then_inc(tfree[b + j], 1)
                elif name.startswith("turn_cat"):
                    i = int(name[-1])
                    await_read(dve, tfree, tail_u[f"z{i}"])
                    for j in range(2):
                        await_bank(dve, "tail", u, j)
                        k = 4 * i + 2 * j
                        if i == 0:
                            ins = V.scalar_tensor_tensor(szt[:, k:k + 2, :], bank(b + j, c=2, s=SEQ), sub_gain, szt[:, k:k + 2, :], ALU.mult, ALU.mult)
                        else:
                            ins = V.tensor_tensor(szt[:, k:k + 2, :], bank(b + j, c=2, s=SEQ), szt[:, k:k + 2, :], ALU.mult)
                        ins.then_inc(tfree[b + j], 1)
                    for j in range(2):
                        k = 4 * i + 2 * j
                        dve.wait_ge(yt_hi_ready, k // 2 + 1)
                        rest(ht_lo[:, k:k + 2, :], szt[:, k:k + 2, :], ht_hi[:, k:k + 2, :], yt_ready)
                split_ahead(ahead_late.get(name, ()))
                if name in SCORES_AFTER:
                    score_max(SCORES_AFTER[name])
                if name in ("v_diff", "v_dil"):
                    diff_weights(("v_diff", "v_dil").index(name))
            split_ahead([first_slot["w_out"] + 3, first_slot["w_gate"], first_slot["w_gate"] + 1])
            dve.wait_ge(slot_used, first_slot["w_out"] + 4)
            for n in range(2):
                for tt in range(TT):
                    cols = slice(n * BANK, (n + 1) * BANK)
                    V.tensor_tensor(x[:, tt, cols], x[:, tt, cols], bank(4 + 2 * tt + n), ALU.add).then_inc(x_ready, 1)
            dve.wait_ge(x_ready, 14)
            split_norm(0, col[:, C_PLE:C_PLE + KD], 8)
            norm_rows(4, halves=1)
            split_ahead([first_slot["w_gate"] + 2, first_slot["w_gate"] + 3])
            for c in range(4):
                cols = slice(c * HALF, (c + 1) * HALF)
                for tt in range(TT):
                    dve.wait_ge(gate_sig, 2 * c + tt + 1)
                    link(V.tensor_tensor(gt[:, tt, cols], gt[:, tt, cols], pp[:, tt, cols], ALU.mult))
                    V.tensor_tensor(x[:, tt, cols], x[:, tt, cols], gt[:, tt, cols], ALU.add).then_inc(out_ready, 1)


def vec_sources(t):
    found = [(C_C, t["c"].rearrange("b (k p) -> (b k) p", p=P))]
    for at, name in ((C_GMIX, "g_norm_mix"), (C_GMOE, "g_norm_moe"), (C_MIX2, "mix_norm_g_2"), (C_PLE, "ple_norm_g_2"),
                     (C_BADA, "b_ada"), (C_BGATE, "b_gate")):
        found.append((at, t[name].rearrange("b (k p) -> (b k) p", p=P)))
    found.append((C_CONV, t["w_conv"][0].rearrange("w (k p) -> (w k) p", p=P)))
    return found


VEC_DMAS = 8

_INS = ["x", "c", "w_ada", "b_ada", "g_norm_mix", "w_in", "b_gate", "w_fourier", "w_conv", "w_conv_out", "w_o",
        "g_norm_moe", "w_router", "b_router", "w_gate_e", "w_up_e", "w_down_e", "g_final", "p_2", "mix_norm_g_2",
        "w_in_2", "diff_q_norm_g_2", "diff_k_norm_g_2", "lambda_q1_2", "lambda_k1_2", "lambda_q2_2", "lambda_k2_2",
        "diff_sub_norm_g_2", "dil_q_norm_g_2", "dil_k_norm_g_2", "w_out_2", "ple_norm_g_2", "w_ple_gate_2",
        "w_ple_proj_2"]


def kernel(**inputs):
    import concourse.bacc as bacc
    from concourse.bass_utils import run_bass_kernel_spmd

    nc = bacc.Bacc("TRN2", target_bir_lowering=False, num_devices=1)
    arrays, tensors = {}, {}
    for name, a in list({n: inputs[n] for n in _INS}.items()) + list(shape_constants().items()):
        a = np.ascontiguousarray(a)
        arrays[f"in_{name}"] = a
        tensors[name] = nc.dram_tensor(f"in_{name}", a.shape, mybir.dt.from_np(a.dtype), kind="ExternalInput").ap()
    out = nc.dram_tensor("out", (1, SEQ, D), F32, kind="ExternalOutput").ap()
    build(nc, tensors, out)
    return run_bass_kernel_spmd(nc, [arrays], core_ids=[0]).results[0]["out"]
```
